# Optimizing a Trainium2 kernel written in Bass

```python
import math
import jax
import jax.numpy as jnp
from jax import lax
import numpy as np

D_MODEL = 1024
BATCH = 1
SEQ = 1024
DEPTH = 2

GRID_W = 64
CTX_LEN = 256
HEAD_DIM = 64
ROPE_THETA = 10000.0
Q_BLOCK = 128
RMS_EPS = 1e-6
SUBLN_EPS = 1e-5

A_HEADS = D_MODEL // (2 * HEAD_DIM)
A_KV_HEADS = A_HEADS // 4
A_WIDTH = A_HEADS * HEAD_DIM
A_KV_WIDTH = A_KV_HEADS * HEAD_DIM
A_COLS = A_WIDTH + 2 * A_KV_WIDTH

B_HEADS = D_MODEL // (2 * HEAD_DIM)
B_WIDTH = B_HEADS * HEAD_DIM
RWKV_W_LORA = 64
RWKV_A_LORA = 64
RWKV_V_LORA = 32
RWKV_G_LORA = 128
RWKV_GN_EPS = 64e-5
DECAY_SCALE = math.exp(-0.5)
B_SPLITS = (B_WIDTH, 2 * B_WIDTH, 3 * B_WIDTH, 3 * B_WIDTH + RWKV_W_LORA,
            3 * B_WIDTH + RWKV_W_LORA + RWKV_A_LORA)
B_COLS = 3 * B_WIDTH + RWKV_W_LORA + RWKV_A_LORA + RWKV_G_LORA
EVEN_COLS = A_COLS + B_COLS

C_HEADS = D_MODEL // (2 * HEAD_DIM)
C_QK = C_HEADS * 2 * HEAD_DIM
ODD_COLS = 2 * C_QK + C_HEADS * 2 * HEAD_DIM

N_GROUPS = 4
EXPERTS_PER_GROUP = 8
N_EXPERTS = N_GROUPS * EXPERTS_PER_GROUP
TOP_K = 2
EXPERT_HIDDEN = D_MODEL // 2
EXPERT_BLOCK = 128

N_EVEN = (DEPTH + 1) // 2
N_ODD = DEPTH // 2

kernel_name = 'hybrid_gqa_rwkv7_diffattn_hmoe_dit'

def rms_norm(x, gain=None, eps=RMS_EPS):
    xf = x.astype(jnp.float32)
    y = xf * lax.rsqrt(jnp.mean(xf * xf, axis=-1, keepdims=True) + eps)
    if gain is not None:
        y = y * gain.astype(jnp.float32)
    return y.astype(x.dtype)

def modulate(h, shift, scale):
    return h * (1.0 + scale) + shift

def axial_rope_tables(rows):
    nf = HEAD_DIM // 4
    inv = ROPE_THETA ** (-jnp.arange(nf, dtype=jnp.float32) / nf)
    r_idx = jnp.repeat(jnp.arange(rows, dtype=jnp.float32), GRID_W)
    c_idx = jnp.tile(jnp.arange(GRID_W, dtype=jnp.float32), rows)
    ang = jnp.concatenate([r_idx[:, None] * inv, c_idx[:, None] * inv], axis=-1)
    return jnp.cos(ang), jnp.sin(ang)

def apply_axial_rope(x, cos, sin):
    shp = x.shape
    nf = shp[-1] // 4
    n_head_axes = x.ndim - 3
    xr = x.astype(jnp.float32).reshape(*shp[:-1], 2, 2, nf)
    cs = cos.reshape(cos.shape[0], *([1] * n_head_axes), 2, nf)
    sn = sin.reshape(sin.shape[0], *([1] * n_head_axes), 2, nf)
    x1, x2 = xr[..., 0, :], xr[..., 1, :]
    out = jnp.stack([x1 * cs - x2 * sn, x1 * sn + x2 * cs], axis=-2)
    return out.reshape(shp).astype(x.dtype)

def sweep_query_blocks(attend, q):
    b, t = q.shape[:2]
    nblk = t // Q_BLOCK
    qb = jnp.moveaxis(q.reshape(b, nblk, Q_BLOCK, *q.shape[2:]), 1, 0)
    ob = jnp.moveaxis(lax.map(attend, qb), 0, 1)
    return ob.reshape(b, t, *ob.shape[3:])

def gqa_project(pa, q_gain, k_gain):
    b, t, _ = pa.shape
    q = pa[..., :A_WIDTH].reshape(b, t, A_KV_HEADS, A_HEADS // A_KV_HEADS, HEAD_DIM)
    k = pa[..., A_WIDTH:A_WIDTH + A_KV_WIDTH].reshape(b, t, A_KV_HEADS, HEAD_DIM)
    v = pa[..., A_WIDTH + A_KV_WIDTH:].reshape(b, t, A_KV_HEADS, HEAD_DIM)
    return rms_norm(q, q_gain), rms_norm(k, k_gain), v

def gqa_attend(q, k, v):
    s = jnp.einsum('bqhgd,bkhd->bhgqk', q, k, preferred_element_type=jnp.float32) * HEAD_DIM ** -0.5
    p = jax.nn.softmax(s, axis=-1).astype(v.dtype)
    return jnp.einsum('bhgqk,bkhd->bqhgd', p, v)

def token_shift(u, mu_prev, mu_next):
    zero = jnp.zeros_like(u[:, :1])
    prev = jnp.concatenate([zero, u[:, :-1]], axis=1)
    nxt = jnp.concatenate([u[:, 1:], zero], axis=1)
    return u + mu_prev * (prev - u) + mu_next * (nxt - u)

def rwkv_prepare(u, v_first, p):
    b, t, _ = u.shape
    u = token_shift(u, p['mu_prev'], p['mu_next'])
    r, k, v, wlr, alr, glr = jnp.split(u, B_SPLITS, axis=-1)
    if v_first is None:
        v_first = v
    else:
        v = v + (v_first - v) * jax.nn.sigmoid(p['v0'] + (v @ p['v1']) @ p['v2'])
    heads = lambda z: z.astype(jnp.float32).reshape(b, t, B_HEADS, HEAD_DIM)
    kk = heads(k * p['k_k'])
    kk = kk / jnp.maximum(jnp.linalg.norm(kk, axis=-1, keepdims=True), 1e-12)
    k_a = p['k_a'].astype(jnp.float32).reshape(B_HEADS, HEAD_DIM)
    tw = jnp.tanh(wlr)
    dirs = []
    for dr in range(2):
        w = jnp.exp(-DECAY_SCALE * jax.nn.sigmoid(heads(p['w0'][dr] + tw @ p['w2'][dr])))
        a = jax.nn.sigmoid(heads(p['a0'][dr] + alr @ p['a2'][dr]))
        kd = heads(k) * (1.0 + (a - 1.0) * k_a)
        dirs.append({'w': w, 'a': a, 'k': kd})
    g = jax.nn.sigmoid(glr) @ p['g2']
    return {'r': heads(r), 'v': heads(v), 'kk': kk, 'g': g, 'dirs': dirs}, v_first

def delta_scan(s0, seq, dr, reverse):
    dd = seq['dirs'][dr]
    xs = tuple(jnp.moveaxis(z, 1, 0) for z in (seq['r'], dd['w'], dd['k'], seq['v'], seq['kk'], dd['a']))

    def step(s, inp):
        r_t, w_t, k_t, v_t, kk_t, a_t = inp
        s_kk = jnp.einsum('bhvk,bhk->bhv', s, kk_t)
        s = (s * w_t[:, :, None, :] - s_kk[..., None] * (kk_t * a_t)[:, :, None, :]
             + v_t[..., None] * k_t[:, :, None, :])
        return s, jnp.einsum('bhvk,bhk->bhv', s, r_t)

    s_last, ys = lax.scan(step, s0, xs, reverse=reverse)
    return s_last, jnp.moveaxis(ys, 0, 1)

def rwkv_readout(y, seq, p):
    b, t = y.shape[:2]
    mu = jnp.mean(y, axis=-1, keepdims=True)
    var = jnp.mean(jnp.square(y - mu), axis=-1, keepdims=True)
    gn_w = p['gn_w'].astype(jnp.float32).reshape(B_HEADS, HEAD_DIM)
    gn_b = p['gn_b'].astype(jnp.float32).reshape(B_HEADS, HEAD_DIM)
    y = (y - mu) * lax.rsqrt(var + RWKV_GN_EPS) * gn_w + gn_b
    r_k = p['r_k'].astype(jnp.float32)
    for dd in seq['dirs']:
        y = y + jnp.sum(seq['r'] * dd['k'] * r_k, axis=-1, keepdims=True) * seq['v']
    g = seq['g']
    return (y.reshape(b, t, B_WIDTH) * g.astype(jnp.float32)).astype(g.dtype)

def rwkv_mix(u_lat, u_ctx, v_first, p):
    vf_lat, vf_ctx = (None, None) if v_first is None else v_first
    lat, vf_lat = rwkv_prepare(u_lat, vf_lat, p)
    ctx, vf_ctx = rwkv_prepare(u_ctx, vf_ctx, p)
    s0 = jnp.zeros((u_lat.shape[0], B_HEADS, HEAD_DIM, HEAD_DIM), jnp.float32)
    y_lat = 0.0
    y_ctx = 0.0
    for dr, reverse in enumerate((False, True)):
        s_ctx, yc = delta_scan(s0, ctx, dr, reverse)
        _, yl = delta_scan(s_ctx, lat, dr, reverse)
        y_lat = y_lat + yl
        y_ctx = y_ctx + yc
    return rwkv_readout(y_lat, lat, p), rwkv_readout(y_ctx, ctx, p), (vf_lat, vf_ctx)

def even_mixer(hl, hc, v_first, p, cos, sin):
    b, t, _ = hl.shape
    pl = hl @ p['w_in']
    pc = hc @ p['w_in']
    ql, kl, vl = gqa_project(pl[..., :A_COLS], p['q_gain'], p['k_gain'])
    qc, kc, vc = gqa_project(pc[..., :A_COLS], p['q_gain'], p['k_gain'])
    ql = apply_axial_rope(ql, cos, sin)
    kl = apply_axial_rope(kl, cos, sin)
    k_all = jnp.concatenate([kc, kl], axis=1)
    v_all = jnp.concatenate([vc, vl], axis=1)
    al = sweep_query_blocks(lambda qb: gqa_attend(qb, k_all, v_all), ql).reshape(b, t, A_WIDTH)
    ac = gqa_attend(qc, kc, vc).reshape(b, hc.shape[1], A_WIDTH)
    bl, bc, v_first = rwkv_mix(pl[..., A_COLS:], pc[..., A_COLS:], v_first, p)
    out_l = jnp.concatenate([al, bl], axis=-1) @ p['w_out']
    out_c = jnp.concatenate([ac, bc], axis=-1) @ p['w_out']
    return out_l, out_c, v_first

def diff_attend(q, k, v, lam):
    s = jnp.einsum('bqhcd,bkhcd->bhcqk', q, k, preferred_element_type=jnp.float32) * HEAD_DIM ** -0.5
    pr = jax.nn.softmax(s, axis=-1)
    pr = pr[:, :, 0] - lam * pr[:, :, 1]
    return jnp.einsum('bhqk,bkhe->bqhe', pr.astype(v.dtype), v)

def diff_mixer(hl, hc, p, lambda_init, cos, sin, need_ctx):
    def split_q(z):
        return z.reshape(*z.shape[:2], C_HEADS, 2, HEAD_DIM)

    def split_kv(z):
        k = z[..., :C_QK].reshape(*z.shape[:2], C_HEADS, 2, HEAD_DIM)
        v = z[..., C_QK:].reshape(*z.shape[:2], C_HEADS, 2 * HEAD_DIM)
        return k, v

    def finish(o):
        o = rms_norm(o, p['subln'], SUBLN_EPS) * (1.0 - lambda_init)
        return o.reshape(*o.shape[:2], C_HEADS * 2 * HEAD_DIM) @ p['w_out']

    pl = hl @ p['w_in']
    ql = apply_axial_rope(split_q(pl[..., :C_QK]), cos, sin)
    kl, vl = split_kv(pl[..., C_QK:])
    kl = apply_axial_rope(kl, cos, sin)
    kc, vc = split_kv(hc @ p['w_in'][:, C_QK:])
    f32 = jnp.float32
    lam = (jnp.exp(jnp.sum(p['lq1'].astype(f32) * p['lk1'].astype(f32)))
           - jnp.exp(jnp.sum(p['lq2'].astype(f32) * p['lk2'].astype(f32))) + lambda_init)
    k_all = jnp.concatenate([kc, kl], axis=1)
    v_all = jnp.concatenate([vc, vl], axis=1)
    out_l = finish(sweep_query_blocks(lambda qb: diff_attend(qb, k_all, v_all, lam), ql))
    if not need_ctx:
        return out_l, None
    qc = split_q(hc @ p['w_in'][:, :C_QK])
    return out_l, finish(diff_attend(qc, kc, vc, lam))

def grouped_expert_mlp(h, expert_id, w_gate, w_up, w_down):
    n, d = h.shape
    k = expert_id.shape[1]
    m = n * k
    e_flat = expert_id.reshape(m)
    tok = jnp.arange(m, dtype=jnp.int32) // k
    counts = jnp.bincount(e_flat, length=N_EXPERTS).astype(jnp.int32)
    padded = (counts + EXPERT_BLOCK - 1) // EXPERT_BLOCK * EXPERT_BLOCK
    pad_end = jnp.cumsum(padded)
    pad_start = pad_end - padded
    raw_start = jnp.cumsum(counts) - counts
    order = jnp.argsort(e_flat)
    e_sorted = e_flat[order]
    slot_sorted = pad_start[e_sorted] + jnp.arange(m, dtype=jnp.int32) - raw_start[e_sorted]
    n_blocks = -(-(m + N_EXPERTS * (EXPERT_BLOCK - 1)) // EXPERT_BLOCK)
    slot_tok = jnp.full((n_blocks * EXPERT_BLOCK,), n, jnp.int32).at[slot_sorted].set(tok[order])
    block_start = jnp.arange(n_blocks, dtype=jnp.int32) * EXPERT_BLOCK
    block_expert = jnp.minimum(jnp.searchsorted(pad_end, block_start, side='right'), N_EXPERTS - 1)
    h_pad = jnp.concatenate([h, jnp.zeros((1, d), h.dtype)], axis=0)
    xb = h_pad[slot_tok].reshape(n_blocks, EXPERT_BLOCK, d)

    def run_block(args):
        xblk, e = args
        return (jax.nn.silu(xblk @ w_gate[e]) * (xblk @ w_up[e])) @ w_down[e]

    yb = lax.map(run_block, (xb, block_expert)).reshape(n_blocks * EXPERT_BLOCK, d)
    slot = jnp.zeros((m,), jnp.int32).at[order].set(slot_sorted)
    return yb[slot].reshape(n, k, d)

def moe_ffn(h, w_grp, b_grp, w_rt, b_rt, w_gate, w_up, w_down):
    n = h.shape[0]
    f32 = jnp.float32
    hf = h.astype(f32)
    grp_logits = hf @ w_grp.astype(f32) + b_grp.astype(f32)
    grp_sel = jnp.argmax(grp_logits, axis=-1)
    grp_w = jnp.take_along_axis(jax.nn.softmax(grp_logits, axis=-1), grp_sel[:, None], axis=1)
    exp_logits = (hf @ w_rt.astype(f32) + b_rt.astype(f32)).reshape(n, N_GROUPS, EXPERTS_PER_GROUP)
    exp_logits = jnp.take_along_axis(exp_logits, grp_sel[:, None, None], axis=1)[:, 0]
    top_p, top_i = lax.top_k(jax.nn.softmax(exp_logits, axis=-1), TOP_K)
    gates = grp_w * top_p / jnp.sum(top_p, axis=-1, keepdims=True)
    expert_id = (grp_sel[:, None] * EXPERTS_PER_GROUP + top_i).astype(jnp.int32)
    y = grouped_expert_mlp(h, expert_id, w_gate, w_up, w_down)
    return jnp.einsum('nk,nkd->nd', gates.astype(h.dtype), y)

def setup_inputs(seed: int = 0) -> dict:
    key = jax.random.key(seed)
    ks = iter(jax.random.split(key, 48))
    d = D_MODEL

    def nrm(shape, scale=1.0):
        return scale * jax.random.normal(next(ks), shape, jnp.float32)

    def unif(shape, lo, hi):
        return jax.random.uniform(next(ks), shape, jnp.float32, lo, hi)

    return {
        'x': nrm((BATCH, SEQ, d)),
        'c': nrm((BATCH, d)),
        'ctx': nrm((BATCH, CTX_LEN, d)),
        'c_ctx': nrm((d,)),
        'mod_w': nrm((DEPTH, d, 6 * d), 0.3 * d ** -0.5),
        'mod_b': nrm((DEPTH, 6 * d), 0.02),
        'ev_w_in': nrm((N_EVEN, d, EVEN_COLS), d ** -0.5),
        'ev_w_out': nrm((N_EVEN, A_WIDTH + B_WIDTH, d), (A_WIDTH + B_WIDTH) ** -0.5),
        'ev_q_gain': 1.0 + nrm((N_EVEN, HEAD_DIM), 0.05),
        'ev_k_gain': 1.0 + nrm((N_EVEN, HEAD_DIM), 0.05),
        'ev_mu_prev': unif((N_EVEN, B_COLS), 0.0, 0.5),
        'ev_mu_next': unif((N_EVEN, B_COLS), 0.0, 0.5),
        'ev_w0': -1.0 + nrm((N_EVEN, 2, B_WIDTH), 0.5),
        'ev_w2': nrm((N_EVEN, 2, RWKV_W_LORA, B_WIDTH), 0.5 * RWKV_W_LORA ** -0.5),
        'ev_a0': nrm((N_EVEN, 2, B_WIDTH), 0.5),
        'ev_a2': nrm((N_EVEN, 2, RWKV_A_LORA, B_WIDTH), 0.5 * RWKV_A_LORA ** -0.5),
        'ev_g2': nrm((N_EVEN, RWKV_G_LORA, B_WIDTH), RWKV_G_LORA ** -0.5),
        'ev_k_k': 0.85 + nrm((N_EVEN, B_WIDTH), 0.05),
        'ev_k_a': 1.0 + nrm((N_EVEN, B_WIDTH), 0.05),
        'ev_r_k': nrm((N_EVEN, B_HEADS, HEAD_DIM), 0.1),
        'ev_gn_w': 1.0 + nrm((N_EVEN, B_WIDTH), 0.05),
        'ev_gn_b': nrm((N_EVEN, B_WIDTH), 0.02),
        'ev_v0': nrm((N_EVEN - 1, B_WIDTH), 0.5),
        'ev_v1': nrm((N_EVEN - 1, B_WIDTH, RWKV_V_LORA), B_WIDTH ** -0.5),
        'ev_v2': nrm((N_EVEN - 1, RWKV_V_LORA, B_WIDTH), RWKV_V_LORA ** -0.5),
        'od_w_in': nrm((N_ODD, d, ODD_COLS), d ** -0.5),
        'od_w_out': nrm((N_ODD, C_HEADS * 2 * HEAD_DIM, d), d ** -0.5),
        'od_lq1': nrm((N_ODD, HEAD_DIM), 0.1),
        'od_lk1': nrm((N_ODD, HEAD_DIM), 0.1),
        'od_lq2': nrm((N_ODD, HEAD_DIM), 0.1),
        'od_lk2': nrm((N_ODD, HEAD_DIM), 0.1),
        'od_subln': 1.0 + nrm((N_ODD, 2 * HEAD_DIM), 0.05),
        'moe_w_grp': nrm((DEPTH, d, N_GROUPS), d ** -0.5),
        'moe_b_grp': nrm((DEPTH, N_GROUPS), 0.01),
        'moe_w_rt': nrm((DEPTH, d, N_EXPERTS), d ** -0.5),
        'moe_b_rt': nrm((DEPTH, N_EXPERTS), 0.01),
        'moe_w_gate': nrm((DEPTH, N_EXPERTS, d, EXPERT_HIDDEN), d ** -0.5),
        'moe_w_up': nrm((DEPTH, N_EXPERTS, d, EXPERT_HIDDEN), d ** -0.5),
        'moe_w_down': nrm((DEPTH, N_EXPERTS, EXPERT_HIDDEN, d), EXPERT_HIDDEN ** -0.5),
        'final_gain': 1.0 + nrm((d,), 0.05),
    }

def reference(x, c, ctx, c_ctx, mod_w, mod_b, ev_w_in, ev_w_out, ev_q_gain, ev_k_gain,
              ev_mu_prev, ev_mu_next, ev_w0, ev_w2, ev_a0, ev_a2, ev_g2, ev_k_k, ev_k_a, ev_r_k,
              ev_gn_w, ev_gn_b, ev_v0, ev_v1, ev_v2, od_w_in, od_w_out, od_lq1, od_lk1, od_lq2,
              od_lk2, od_subln, moe_w_grp, moe_b_grp, moe_w_rt, moe_b_rt, moe_w_gate, moe_w_up,
              moe_w_down, final_gain):
    bsz, n_lat, d = x.shape
    rows = n_lat // GRID_W
    cos, sin = axial_rope_tables(rows)
    cond_lat = jax.nn.silu(c)
    cond_ctx = jax.nn.silu(c_ctx)[None, :]
    xc = ctx
    v_first = None
    for layer in range(DEPTH):
        last = layer == DEPTH - 1
        mods_l = jnp.split((cond_lat @ mod_w[layer] + mod_b[layer])[:, None, :], 6, axis=-1)
        mods_c = jnp.split((cond_ctx @ mod_w[layer] + mod_b[layer])[:, None, :], 6, axis=-1)
        hl = modulate(rms_norm(x), mods_l[0], mods_l[1])
        hc = modulate(rms_norm(xc), mods_c[0], mods_c[1])
        if layer % 2 == 0:
            e = layer // 2
            p = {'w_in': ev_w_in[e], 'w_out': ev_w_out[e], 'q_gain': ev_q_gain[e],
                 'k_gain': ev_k_gain[e], 'mu_prev': ev_mu_prev[e], 'mu_next': ev_mu_next[e],
                 'w0': ev_w0[e], 'w2': ev_w2[e], 'a0': ev_a0[e], 'a2': ev_a2[e], 'g2': ev_g2[e],
                 'k_k': ev_k_k[e], 'k_a': ev_k_a[e], 'r_k': ev_r_k[e], 'gn_w': ev_gn_w[e],
                 'gn_b': ev_gn_b[e]}
            if e > 0:
                p['v0'] = ev_v0[e - 1]
                p['v1'] = ev_v1[e - 1]
                p['v2'] = ev_v2[e - 1]
            out_l, out_c, v_first = even_mixer(hl, hc, v_first, p, cos, sin)
        else:
            o = layer // 2
            p = {'w_in': od_w_in[o], 'w_out': od_w_out[o], 'lq1': od_lq1[o], 'lk1': od_lk1[o],
                 'lq2': od_lq2[o], 'lk2': od_lk2[o], 'subln': od_subln[o]}
            lambda_init = 0.8 - 0.6 * math.exp(-0.3 * layer)
            out_l, out_c = diff_mixer(hl, hc, p, lambda_init, cos, sin, not last)
        x = x + mods_l[2] * out_l
        hl = modulate(rms_norm(x), mods_l[3], mods_l[4])
        moe_p = (moe_w_grp[layer], moe_b_grp[layer], moe_w_rt[layer], moe_b_rt[layer],
                 moe_w_gate[layer], moe_w_up[layer], moe_w_down[layer])
        if last:
            x = x + mods_l[5] * moe_ffn(hl.reshape(-1, d), *moe_p).reshape(x.shape)
        else:
            xc = xc + mods_c[2] * out_c
            hc = modulate(rms_norm(xc), mods_c[3], mods_c[4])
            n_ctx = hc.shape[0] * hc.shape[1]
            y = moe_ffn(jnp.concatenate([hc.reshape(-1, d), hl.reshape(-1, d)], axis=0), *moe_p)
            xc = xc + mods_c[5] * y[:n_ctx].reshape(xc.shape)
            x = x + mods_l[5] * y[n_ctx:].reshape(x.shape)
    return rms_norm(x, final_gain)


_drawn_inputs = setup_inputs


def setup_inputs(seed=0):
    import zlib

    import numpy as np

    out = dict(_drawn_inputs(seed))
    spreads = {}
    factors = {'ev_q_gain': 8.0,
     'ev_k_gain': 8.0,
     'ev_w0': 3.186,
     'ev_w2': 8.0,
     'ev_a0': 3.329,
     'ev_a2': 4.775,
     'ev_k_k': 135.693,
     'ev_k_a': 8.0,
     'ev_r_k': 2.827,
     'ev_gn_w': 8.0,
     'ev_gn_b': 8.0,
     'od_lq1': 3.163,
     'od_lk1': 3.776,
     'od_lq2': 4.303,
     'od_lk2': 200.0,
     'od_subln': 7.466,
     'moe_b_grp': 56.064,
     'moe_b_rt': 49.536}
    for name, (base, spread) in spreads.items():
        noise = np.random.default_rng([zlib.crc32(name.encode()), seed]).standard_normal(out[name].shape)
        drawn = base * np.exp(spread * noise) if base else spread * noise
        out[name] = jnp.asarray(drawn.astype(out[name].dtype))
    for name, factor in factors.items():
        out[name] = (out[name] * factor).astype(out[name].dtype)
    return out
```

```python
import math
from contextlib import ExitStack

import numpy as np
import concourse.bass as bass
from concourse import mybir

F32 = mybir.dt.float32
F32R = mybir.dt.float32r
U32 = mybir.dt.uint32
I32 = mybir.dt.int32
ALU = mybir.AluOpType
ACT = mybir.ActivationFunctionType
AX = mybir.AxisListType
ds = bass.ds

P = 128
D = 1024
KT = D // P
SEQ, CTX = 1024, 256
TOK = SEQ + CTX
NT = TOK // P
CT = CTX // P
HD = 64
GRID_W = 64
ROPE_THETA = 10000.0
RMS_EPS, SUBLN_EPS, GN_EPS = 1e-6, 1e-5, 64e-5
AH, AKV = 8, 2
AW, AKW = AH * HD, AKV * HD
A_COLS = AW + 2 * AKW
BH = 8
BW = BH * HD
B_COLS = 3 * BW + 64 + 64 + 128
DECAY = math.exp(-0.5)
CH = 8
NG, EPG, NE = 4, 8, 32
EH = D // 2
MODS = 6 * D
SHIFT1, SCALE1, GATE1, SHIFT2, SCALE2, GATE2 = range(6)


class Scope:

    def __init__(self, nc, ctx, sems, tag):
        self.nc, self.ctx, self.tag, self.mine = nc, ctx, tag, []
        ctx.callback(self.close)

    def sb(self, name, shape, dt=F32):
        return self.ctx.enter_context(self.nc.sbuf_tensor(f"{self.tag}_{name}", shape, dt))

    def ps(self, name, shape=(P, 512), dt=F32):
        return self.ctx.enter_context(self.nc.psum_tensor(f"{self.tag}_{name}", list(shape), dt))

    def sem(self, name):
        self.mine.append(self.nc.alloc_semaphore(f"{self.tag}_{name}"))
        return self.mine[-1]

    def close(self):
        self.nc.clear_and_free_semaphores(self.mine)
        self.nc.all_engine_barrier()


class Steps:

    def __init__(self, sem, base=0):
        self.sem, self.base, self.n = sem, base, 0

    def did(self, ins, by=1):
        ins.then_inc(self.sem, by)
        self.n += by
        return self.base + self.n


def mods_phase(nc, sems, d, rows_):
    RING, NCH = 4, MODS // 512
    with ExitStack() as ctx:
        s = Scope(nc, ctx, sems, "mods")
        cond = s.sb("cond", [P, 2, KT])
        sil = s.sb("sil", [P, KT, 2])
        bias = s.sb("bias", [2, 2, MODS])
        rows = s.sb("rows", [2, 2, MODS])
        w = s.sb("w", [P, RING, KT, 512])
        acc = [s.ps(f"acc{u}") for u in range(RING)]
        cond_in, bias_in, sil_done, out_done = s.sem("cond_in"), s.sem("bias_in"), s.sem("sil_done"), s.sem("out")
        w_in = [s.sem(f"w_in{u}") for u in range(RING)]
        mm_done, acc_free, rows_in = s.sem("mm_done"), s.sem("acc_free"), s.sem("rows_in")

        with nc.Block() as block:
            @block.sync
            def _(sp):
                sp.dma_start(cond[:, 0, :], d["c"].rearrange("a (p k) -> p (a k)", k=KT)).then_inc(cond_in, 16)
                sp.dma_start(cond[:, 1, :], d["c_ctx"].rearrange("(p k) -> p k", k=KT)).then_inc(cond_in, 16)
                for c in range(2):
                    sp.dma_start(bias[c:c + 1, :, :], d["mod_b"].rearrange("(o l) n -> o l n", o=1)).then_inc(bias_in, 16)
                for l in range(2):
                    src = d["mod_w"][l].rearrange("(p k) n -> p k n", k=KT)
                    with sp.Fori(0, NCH // RING) as i:
                        for u in range(RING):
                            sp.wait_ge(mm_done, RING * (i + (NCH // RING) * l) + u + 1)
                            sp.dma_start(w[:, u, :, :], src[:, :, ds(i * (RING * 512) + u * 512, 512)]).then_inc(w_in[u], 16)
                sp.wait_ge(acc_free, RING + 2 * NCH)
                sp.dma_start(d["mods"].rearrange("l c n -> c l n"), rows[:, :, :]).then_inc(out_done, 16)
                sp.wait_ge(out_done, 16)

            @block.scalar
            def _(act):
                act.dma_start(rows_[0:CTX, :], d["ctx"][0]).then_inc(rows_in, 16)
                act.dma_start(rows_[CTX:TOK, :], d["x"][0]).then_inc(rows_in, 16)
                act.wait_ge(rows_in, 32)
                act.wait_ge(cond_in, 32)
                nc.scalar.activation(sil[:, :, :], cond[:, :, :].rearrange("p c k -> p k c"), ACT.Silu).then_inc(sil_done, 1)

            @block.tensor
            def _(pe):
                pe.sem_inc(mm_done, RING)
                pe.wait_ge(sil_done, 1)
                for l in range(2):
                    with pe.Fori(0, NCH // RING) as i:
                        for u in range(RING):
                            n = RING * (i + (NCH // RING) * l) + u
                            pe.wait_ge(w_in[u], 16 * (i + (NCH // RING) * l + 1))
                            pe.wait_ge(acc_free, n + 1)
                            for k in range(KT):
                                mm = nc.tensor.matmul(acc[u][0:2, :], sil[:, k, :], w[:, u, k, :], start=k == 0, stop=k == KT - 1)
                            mm.then_inc(mm_done, 1)

            @block.vector
            def _(dve):
                dve.sem_inc(acc_free, RING)
                dve.wait_ge(bias_in, 32)
                for l in range(2):
                    with dve.Fori(0, NCH // RING) as i:
                        for u in range(RING):
                            dve.wait_ge(mm_done, RING + RING * (i + (NCH // RING) * l) + u + 1)
                            at = ds(i * (RING * 512) + u * 512, 512)
                            nc.vector.tensor_tensor(rows[:, l, at], acc[u][0:2, :], bias[:, l, at], ALU.add).then_inc(acc_free, 1)


def norm_phase(nc, sems, tag, d, layer, which, src, hT, ident_dram, rows_out=None, first=0):
    tiles = NT - first
    with ExitStack() as ctx:
        s = Scope(nc, ctx, sems, tag)
        ident = s.sb("ident", [P, P])
        mod = s.sb("mod", [P, 2, 2, D])
        x = s.sb("x", [P, 2, D])
        h0 = s.sb("h0", [P, 2, D])
        h = s.sb("h", [P, 2, D])
        sq = s.sb("sq", [P, D])
        ss = s.sb("ss", [P, 2])
        sd = s.sb("sd", [P, 2])
        rstd = s.sb("rstd", [P, 2])
        eps = s.sb("eps", [P, 1])
        tr = [[s.ps(f"tr{u}{b}") for b in range(2)] for u in range(2)]
        const_in, eps_set, scale_done = s.sem("const_in"), s.sem("eps_set"), s.sem("scale_done")
        x_in = [s.sem(f"x_in{u}") for u in range(2)]
        row_out = [s.sem(f"row_out{u}") for u in range(2)]
        act_step, dve_step = s.sem("act_step"), s.sem("dve_step")
        x_free, sd_done, h_done, tr_done, tr_free = s.sem("x_free"), s.sem("sd_done"), s.sem("h_done"), s.sem("tr_done"), s.sem("tr_free")
        split = isinstance(hT, tuple)
        lead, rest = hT if split else (hT, None)
        lead_done = s.sem("lead_done")
        segs = [(cond, a, b) for cond, a, b in ((1, 0, CT // 2), (0, CT // 2, NT // 2)) if 2 * a >= first]

        def pairs(eng, body):
            for cond, a, b in segs:
                if b - a == 1:
                    body(a, a - first // 2, cond)
                else:
                    with eng.Fori(a, b) as j:
                        body(j, j - first // 2, cond)

        with nc.Block() as block:
            @block.sync
            def _(sp):
                sp.dma_start(ident[:, :], ident_dram).then_inc(const_in, 16)
                for c in range(2):
                    for m in range(2):
                        row = d["mods"][layer, c, (which + m) * D:(which + m + 1) * D]
                        sp.dma_start(mod[:, c, m, :], row.rearrange("(o n) -> o n", o=1).to_broadcast([P, D])).then_inc(const_in, 16)

                def body(j, n, cond):
                    for u in range(2):
                        sp.wait_ge(x_free, 2 * n + u + 1)
                        sp.dma_start(x[:, u, :], src[ds(j * (2 * P) + u * P, P), :]).then_inc(x_in[u], 16)
                pairs(sp, body)

            @block.scalar
            def _(act):
                act.wait_ge(eps_set, 1)
                if rows_out is not None:
                    for u in range(2):
                        act.sem_inc(row_out[u], 16)

                def body(j, n, cond):
                    for u in range(2):
                        st = Steps(act_step, 2 * n + u)
                        act.wait_ge(x_in[u], 16 * (n + 1))
                        act.wait_ge(x_free, 2 * n + u + 1)
                        at = st.did(nc.scalar.activation(sq[:, :], x[:, u, :], ACT.Square, accum_out=ss[:, u:u + 1]))
                        act.wait_ge(act_step, at)
                        nc.scalar.activation(sd[:, u:u + 1], ss[:, u:u + 1], ACT.Sqrt, scale=1.0 / D, bias=eps[:, 0:1]).then_inc(sd_done, 1)
                    for u in range(2):
                        if rows_out is not None:
                            act.wait_ge(h_done, 2 * n + u + 1)
                            act.dma_start(rows_out[ds(j * (2 * P) + u * P, P), :], h[:, u, :]).then_inc(row_out[u], 16)
                        for b in range(2):
                            act.wait_ge(tr_done, 4 * n + 2 * u + b + 1)
                            nc.scalar.activation(lead[:, 4 * b:4 * b + 4, ds(j * (2 * P) + u * P, P)],
                                                 tr[u][b][:, :].rearrange("p (k t) -> p k t", k=4), ACT.Copy).then_inc(lead_done if split else tr_free, 1)
                pairs(act, body)
                if rows_out is not None:
                    for u in range(2):
                        act.wait_ge(row_out[u], 16 * (tiles // 2 + 1))

            @block.vector
            def _(dve):
                nc.vector.memset(eps[:, :], RMS_EPS).then_inc(eps_set, 1)
                dve.sem_inc(x_free, 2)
                dve.wait_ge(const_in, 16 * 5)
                for c in range(2):
                    nc.vector.tensor_scalar(mod[:, c, 1, :], mod[:, c, 1, :], 1.0, None, ALU.add).then_inc(scale_done, 1)
                dve.wait_ge(scale_done, 2)

                def body(j, n, cond):
                    for u in range(2):
                        st = Steps(dve_step, 2 * n + u)
                        dve.wait_ge(sd_done, 2 * n + u + 1)
                        at = st.did(nc.vector.reciprocal(rstd[:, u:u + 1], sd[:, u:u + 1]))
                        dve.wait_ge(dve_step, at)
                        nc.vector.scalar_tensor_tensor(out=h0[:, u, :], in0=x[:, u, :], scalar=rstd[:, u:u + 1], in1=mod[:, cond, 1, :],
                                                       op0=ALU.mult, op1=ALU.mult).then_inc(x_free, 1)
                        dve.wait_ge(x_free, 2 + 2 * n + u + 1)
                        dve.wait_ge(tr_free, 4 * n + 2 * u + 2)
                        if rows_out is not None:
                            dve.wait_ge(row_out[u], 16 * (n + 1))
                        nc.vector.tensor_tensor(h[:, u, :], h0[:, u, :], mod[:, cond, 0, :], ALU.add).then_inc(h_done, 1)
                    if split:
                        for u in range(2):
                            for b in range(2):
                                at = (slice(None), slice(4 * b, 4 * b + 4), ds(j * (2 * P) + u * P, P))
                                dve.wait_ge(lead_done, 4 * n + 2 * u + b + 1)
                                nc.vector.tensor_tensor(rest[at], tr[u][b][:, :].rearrange("p (k t) -> p k t", k=4), lead[at].bitcast(F32), ALU.subtract).then_inc(tr_free, 1)
                pairs(dve, body)

            @block.tensor
            def _(pe):
                pe.sem_inc(tr_free, 4)
                pe.wait_ge(const_in, 16 * 5)

                def body(j, n, cond):
                    for u in range(2):
                        pe.wait_ge(h_done, 2 * n + u + 1)
                        for b in range(2):
                            pe.wait_ge(tr_free, 4 * n + 2 * u + b + 1)
                            for k in range(4):
                                kk = 4 * b + k
                                last = nc.tensor.transpose(tr[u][b][:, k * P:(k + 1) * P], h[:, u, kk * P:(kk + 1) * P], ident[:, :])
                            last.then_inc(tr_done, 1)
                pairs(pe, body)


TCH = ((0, 512), (512, 512), (1024, 256))


def proj_phase(nc, sems, tag, w_dram, hT, outT):
    cols = w_dram.shape[1]
    U = 4
    iters = cols // (U * P)
    wv = w_dram.rearrange("(k p) n -> p k n", p=P)
    lead, rest = hT
    with ExitStack() as ctx:
        s = Scope(nc, ctx, sems, tag)
        w = s.sb("w", [P, 2, KT, 2 * P])
        wh, wl = s.sb("wh", [P, 2, KT, 2 * P], F32R), s.sb("wl", [P, 2, KT, 2 * P], F32R)
        o = s.sb("o", [P, 2, TOK])
        acc = [[s.ps(f"acc{u}{c}") for c in range(3)] for u in range(2)]
        w_in = [s.sem(f"w_in{u}") for u in range(2)]
        o_out = [s.sem(f"o_out{u}") for u in range(2)]
        mm_done, dve_ev, act_ev, lead_done, rest_done = (s.sem(n) for n in ("mm_done", "dve_ev", "act_ev", "lead_done", "rest_done"))

        def iterations(eng, body):
            with eng.Fori(0, iters - 1) as i:
                body(i, True)
            body(iters - 1, False)

        with nc.Block() as block:
            @block.sync
            def _(sp):
                with sp.Fori(0, iters) as i:
                    for v in range(2):
                        sp.wait_ge(rest_done, 2 * i + v + 1)
                        sp.dma_start(w[:, v, :, :], wv[:, :, ds(i * (U * P) + v * 2 * P, 2 * P)]).then_inc(w_in[v], 16)

            @block.tensor
            def _(pe):
                pe.sem_inc(mm_done, 3 * U)

                def body(i, more):
                    for u in range(U):
                        if u % 2 == 0:
                            pe.wait_ge(rest_done, 2 + 2 * i + u // 2 + 1)
                        pe.wait_ge(dve_ev, 2 * (U * i + u) + 2)
                        pe.wait_ge(act_ev, U * i + u + 1)
                        at = slice((u % 2) * P, (u % 2 + 1) * P)
                        for c, (t0, n) in enumerate(TCH):
                            for k in range(KT):
                                for x, (a, b) in enumerate(((wh, lead), (wh, rest), (wl, lead))):
                                    mm = nc.tensor.matmul(acc[u % 2][c][:, 0:n], a[:, u // 2, k, at], b[:, k, t0:t0 + n],
                                                          start=k == 0 and x == 0, stop=k == KT - 1 and x == 2)
                            mm.then_inc(mm_done, 1)
                iterations(pe, body)

            @block.vector
            def _(dve):
                dve.sem_inc(dve_ev, 4)
                dve.sem_inc(rest_done, 2)

                def split(i, v):
                    dve.wait_ge(lead_done, 2 * i + v + 1)
                    nc.vector.tensor_tensor(wl[:, v, :, :], w[:, v, :, :], wh[:, v, :, :].bitcast(F32), ALU.subtract).then_inc(rest_done, 1)

                def body(i, more):
                    for u in range(U):
                        dve.wait_ge(o_out[u % 2], 16 * (2 * i + u // 2 + 1))
                        for c in (0, 2):
                            t0, n = TCH[c]
                            dve.wait_ge(mm_done, 3 * (U * (i + 1) + u) + c + 1)
                            nc.vector.tensor_copy(o[:, u % 2, t0:t0 + n], acc[u % 2][c][:, 0:n]).then_inc(dve_ev, 1)
                        if u % 2 == 1 and more:
                            split(i + 1, u // 2)
                for v in range(2):
                    split(0, v)
                iterations(dve, body)

            @block.scalar
            def _(act):
                act.sem_inc(act_ev, 2)
                for u in range(2):
                    act.sem_inc(o_out[u], 16)

                def split(i, v):
                    act.wait_ge(w_in[v], 16 * (i + 1))
                    act.wait_ge(mm_done, 3 * (U * i + 2 * v + 2))
                    nc.scalar.activation(wh[:, v, :, :], w[:, v, :, :], ACT.Copy).then_inc(lead_done, 1)

                def body(i, more):
                    for u in range(U):
                        act.wait_ge(o_out[u % 2], 16 * (2 * i + u // 2 + 1))
                        t0, n = TCH[1]
                        act.wait_ge(mm_done, 3 * (U * (i + 1) + u) + 2)
                        nc.scalar.activation(o[:, u % 2, t0:t0 + n], acc[u % 2][1][:, 0:n], ACT.Copy).then_inc(act_ev, 1)
                        act.wait_ge(act_ev, 2 + U * i + u + 1)
                        act.wait_ge(dve_ev, 4 + 2 * (U * i + u) + 2)
                        act.dma_start(outT[ds(i * (U * P) + u * P, P), :], o[:, u % 2, :]).then_inc(o_out[u % 2], 16)
                        if u % 2 == 1 and more:
                            split(i + 1, u // 2)
                for v in range(2):
                    split(0, v)
                iterations(act, body)
                for u in range(2):
                    act.wait_ge(o_out[u], 16 * (2 * iters + 1))


SWAP16 = [i ^ 16 for i in range(32)]


def qk_phase(nc, sems, tag, d, projT, tiles, vrows, V, gains=None):
    with ExitStack() as ctx:
        s = Scope(nc, ctx, sems, tag)
        cos, sin = s.sb("cos", [P, SEQ]), s.sb("sin", [P, SEQ])
        ident, ones = s.sb("ident", [P, P]), s.sb("ones", [P, P])
        gain = s.sb("gain", [P, 2])
        eps = s.sb("eps", [P, 1])
        x = s.sb("x", [P, 2, TOK])
        sq = s.sb("sq", [P, 2, TOK])
        sd = s.sb("sd", [P, 2, TOK])
        xn = s.sb("xn", [P, 2, TOK])
        sh = s.sb("sh", [P, 2, SEQ])
        ra = s.sb("ra", [P, 2, SEQ])
        vt = s.sb("vt", [P, 2, TOK])
        acc = [[s.ps(f"acc{u}{c}") for c in range(3)] for u in range(2)]
        tr = [s.ps(f"tr{b}") for b in range(2)]
        const_in, eps_set = s.sem("const_in"), s.sem("eps_set")
        x_in = [s.sem(f"x_in{u}") for u in range(2)]
        v_in = [s.sem(f"v_in{u}") for u in range(2)]
        o_out = [s.sem(f"o_out{u}") for u in range(2)]
        sq_done, ss_done, sd_done, xn_done, sh_done, rb_done, o_done = (s.sem(n) for n in (
            "sq_done", "ss_done", "sd_done", "xn_done", "sh_done", "rb_done", "o_done"))
        ra_done, rs_done = s.sem("ra_done"), s.sem("rs_done")
        tr_done, tr_free = s.sem("tr_done"), s.sem("tr_free")
        NB = (NT + 3) // 4

        def loops(eng, body):
            done = 0
            for n, src, dst, g in tiles:
                if n == 2:
                    for u in range(2):
                        body(done, u, src(0, u), dst(0, u), g)
                else:
                    with eng.Fori(0, n // 2) as j:
                        for u in range(2):
                            body(j + done, u, src(j, u), dst(j, u), g)
                done += n // 2
            return done

        with nc.Block() as block:
            @block.sync
            def _(sp):
                sp.dma_start(cos[:, :], d["cos"]).then_inc(const_in, 16)
                sp.dma_start(sin[:, :], d["sin"]).then_inc(const_in, 16)
                sp.dma_start(ident[:, :], d["ident"]).then_inc(const_in, 16)
                sp.dma_start(ones[:, :], d["blockones"]).then_inc(const_in, 16)
                if gains is not None:
                    with nc.allow_non_contiguous_dma(reason="a gain for each channel of a tile, 64 numbers twice"):
                        for g in range(2):
                            for h in range(2):
                                sp.dma_start(gain[h * HD:(h + 1) * HD, g:g + 1], gains[g].rearrange("(p o) -> p o", o=1)).then_inc(const_in, 16)
                for n, v in enumerate(vrows):
                    if n >= 2:
                        sp.wait_ge(tr_free, 2 + NB * (n - 1))
                    sp.dma_start(vt[:, n % 2, :], projT[v * P:(v + 1) * P, :]).then_inc(v_in[n % 2], 16)

                def body(n, u, src, dst, g):
                    sp.wait_ge(xn_done, 2 * n + u + 1)
                    for h, rows in enumerate(src):
                        q = P // len(src)
                        sp.dma_start(x[h * q:(h + 1) * q, u, :], rows).then_inc(x_in[u], 16)
                loops(sp, body)

            nsrc = [len(src(0, 0)) for _, src, _, _ in tiles]
            npairs = [n // 2 for n, _, _, _ in tiles]

            def x_seen(g_index, n):
                before = sum(npairs[:g_index])
                return 16 * (sum(a * b for a, b in zip(nsrc[:g_index], npairs[:g_index])) + (n - before + 1) * nsrc[g_index])

            @block.scalar
            def _(act):
                for u in range(2):
                    act.sem_inc(o_out[u], 16)
                act.wait_ge(eps_set, 1)

                def body(n, u, src, dst, g):
                    if gains is not None:
                        act.wait_ge(x_in[u], x_seen(g, n))
                        act.wait_ge(ss_done, 6 * n + 3 * u + 3)
                        nc.scalar.activation(sq[:, u, :], x[:, u, :], ACT.Square).then_inc(sq_done, 1)
                        for c, (t0, w) in enumerate(TCH):
                            act.wait_ge(ss_done, 6 + 6 * n + 3 * u + c + 1)
                            act.wait_ge(o_done, 2 * n + u + 1)
                            nc.scalar.activation(sd[:, u, t0:t0 + w], acc[u][c][:, 0:w], ACT.Sqrt, scale=1.0, bias=eps[:, 0:1]).then_inc(sd_done, 1)
                    act.wait_ge(o_done, 2 + 2 * n + u + 1)
                    act.dma_start(dst, xn[:, u, :]).then_inc(o_out[u], 16)
                loops(act, body)
                for u in range(2):
                    act.wait_ge(o_out[u], 16 * (1 + sum(npairs)))

            @block.tensor
            def _(pe):
                pe.wait_ge(const_in, 16 * (8 if gains is not None else 4))
                pe.sem_inc(tr_free, 2)
                for n in range(len(vrows)):
                    pe.wait_ge(v_in[n % 2], 16 * (n // 2 + 1))
                    for b in range(NB):
                        pe.wait_ge(tr_free, NB * n + b + 1)
                        for t in range(4 * b, min(4 * b + 4, NT)):
                            last = nc.tensor.transpose(tr[(NB * n + b) % 2][:, (t - 4 * b) * P:(t - 4 * b + 1) * P], vt[:, n % 2, t * P:(t + 1) * P], ident[:, :])
                        last.then_inc(tr_done, 1)
                if gains is not None:
                    pe.sem_inc(ss_done, 6)

                    def body(n, u, src, dst, g):
                        pe.wait_ge(sq_done, 2 * n + u + 1)
                        pe.wait_ge(sd_done, 6 * n + 3 * u + 3)
                        for c, (t0, w) in enumerate(TCH):
                            nc.tensor.matmul(acc[u][c][:, 0:w], ones[:, :], sq[:, u, t0:t0 + w], start=True, stop=True).then_inc(ss_done, 1)
                    loops(pe, body)

            @block.vector
            def _(dve):
                nc.vector.memset(eps[:, :], RMS_EPS).then_inc(eps_set, 1)
                dve.sem_inc(sd_done, 6)
                dve.sem_inc(o_done, 2)
                dve.sem_inc(xn_done, 2)
                dve.wait_ge(const_in, 16 * (8 if gains is not None else 4))
                if gains is not None:
                    nc.vector.tensor_scalar(gain[:, 0:1], gain[:, 0:1], HD ** -0.5, None, ALU.mult).then_inc(eps_set, 1)
                    dve.wait_ge(eps_set, 2)
                for n in range(len(vrows)):
                    for b in range(NB):
                        dve.wait_ge(tr_done, NB * n + b + 1)
                        w = min(4, NT - 4 * b)
                        nc.vector.tensor_copy(V[:, 4 * b:4 * b + w, n * P:(n + 1) * P],
                                              tr[(NB * n + b) % 2][:, 0:w * P].rearrange("p (t c) -> p t c", c=P)).then_inc(tr_free, 1)

                def body(n, u, src, dst, g):
                    dve.wait_ge(o_out[u], 16 * (n + 1))
                    if gains is not None:
                        dve.wait_ge(sd_done, 6 + 6 * n + 3 * u + 3)
                        nc.vector.reciprocal(sd[:, u, :], sd[:, u, :]).then_inc(rs_done, 1)
                        dve.wait_ge(rs_done, 2 * n + u + 1)
                        nc.vector.scalar_tensor_tensor(out=xn[:, u, :], in0=x[:, u, :], scalar=gain[:, g:g + 1], in1=sd[:, u, :], op0=ALU.mult, op1=ALU.mult).then_inc(xn_done, 1)
                    else:
                        dve.wait_ge(x_in[u], x_seen(g, n))
                        nc.vector.tensor_scalar(xn[:, u, :], x[:, u, :], HD ** -0.5 if g == 0 else 1.0, None, ALU.mult).then_inc(xn_done, 1)
                    dve.wait_ge(xn_done, 2 + 2 * n + u + 1)
                    nc.vector.tensor_tensor(ra[:, u, :], xn[:, u, CTX:TOK], cos[:, :], ALU.mult).then_inc(ra_done, 1)
                    nc.vector.stream_shuffle(sh[:, u, :], xn[:, u, CTX:TOK], SWAP16).then_inc(sh_done, 1)
                    dve.wait_ge(ra_done, 2 * n + u + 1)
                    dve.wait_ge(rb_done, 2 * n + u + 1)
                    nc.vector.tensor_tensor(xn[:, u, CTX:TOK], ra[:, u, :], sh[:, u, :], ALU.add).then_inc(o_done, 1)
                loops(dve, body)

            @block.gpsimd
            def _(pool):
                pool.wait_ge(const_in, 16 * (8 if gains is not None else 4))

                def body(n, u, src, dst, g):
                    pool.wait_ge(sh_done, 2 * n + u + 1)
                    nc.gpsimd.tensor_tensor(sh[:, u, :], sh[:, u, :], sin[:, :], ALU.mult).then_inc(rb_done, 1)
                loops(pool, body)


def gqa_qk(nc, sems, d, projT, qT, kT, V):
    def pair(j, u):
        return ds(j * (2 * P) + u * P, P)
    keys = lambda j, u: [projT[AW + u * HD:AW + (u + 1) * HD, :]] * 2
    qk_phase(nc, sems, "gqk", d, projT,
             [(AW // P, lambda j, u: [projT[pair(j, u), :]], lambda j, u: qT[pair(j, u), :], 0),
              (2, keys, lambda j, u: kT[pair(j, u), :], 1)],
             [(AW + AKW) // P], V, gains=[d["ev_q_gain"][0], d["ev_k_gain"][0]])


def attn_phase(nc, sems, tag, d, qT, kmap, K, V, out, pairs, q0, nq, nk, diff):
    LAG = 2 if diff else 1
    RING = 2 * LAG
    W = nk * P
    chunks = [(a, min(512, W - a)) for a in range(0, W, 512)]
    blocks = [list(range(a, min(a + 4, nk))) for a in range(0, nk, 4)]
    groups = [(c, b) for c in range(1 if diff else 2) for b in range(len(blocks))]
    G = len(groups)
    by_act = [True] * G if diff else [g % 2 == 1 for g in range(G)]
    GA, GD = sum(by_act), G - sum(by_act)
    VW = P if diff else HD
    qk_order = [(c, i) for c in range(2) for i in range(len(chunks))]
    per_group = [qk_order[len(qk_order) * g // G:len(qk_order) * (g + 1) // G] for g in range(G)]
    LAMBDA_INIT = 0.8 - 0.6 * math.exp(-0.3)
    with ExitStack() as ctx:
        s = Scope(nc, ctx, sems, tag)
        ident = s.sb("ident", [P, P])
        q = s.sb("q", [P, 2, 2, P])
        p = s.sb("p", [P, RING, 2, W])
        pT = s.sb("pT", [P, G, 512])
        nmax, total, recip = s.sb("nmax", [P, RING, 2]), s.sb("total", [P, RING, 2]), s.sb("recip", [P, RING, 2])
        mix = s.sb("mix", [P, RING])
        o = s.sb("o", [P, 2, P])
        lam = s.sb("lam", [P, 8])
        lqk = s.sb("lqk", [P, 4, HD])
        S = [s.ps(f"S{c}", (P, 1536 if nk > 4 else 512)) for c in range(2)]
        tr, acc = s.ps("tr"), s.ps("acc")
        const_in, q_zero, lam_step, lam_done, lam_exp = (s.sem(n) for n in ("const_in", "q_zero", "lam_step", "lam_done", "lam_exp"))
        q_in = [s.sem(f"q_in{u}") for u in range(2)]
        o_out = [s.sem(f"o_out{u}") for u in range(2)]
        qk_done, nmax_done, p_done, pc_done, r_done = (s.sem(n) for n in ("qk_done", "nmax_done", "p_done", "pc_done", "r_done"))
        tr_done, ev_dve, ev_act, pv_done, o_done, small = (s.sem(n) for n in ("tr_done", "ev_dve", "ev_act", "pv_done", "o_done", "small"))
        TR0 = RING * G

        def units(eng, step):
            def run(pair, first=False):
                for t in range(nq):
                    before = t - LAG
                    late = (None if first else pair - 1) if before < 0 else pair
                    step(pair * nq + t, t, pair, late, True)
            run(0, True)
            if pairs > 1:
                with eng.Fori(1, pairs) as pair:
                    run(pair)
            for t in range(LAG):
                step(pairs * nq + t, t, None, pairs - 1, False)

        with nc.Block() as block:
            @block.sync
            def _(sp):
                sp.dma_start(ident[:, :], d["ident"]).then_inc(const_in, 16)
                if diff:
                    for i, n in enumerate(("od_lq1", "od_lk1", "od_lq2", "od_lk2")):
                        sp.dma_start(lqk[:, i, :], d[n].to_broadcast([P, HD])).then_inc(const_in, 16)
                sp.wait_ge(q_zero, 1)

                def step(n, t, pair, late, scores):
                    if scores:
                        sp.wait_ge(qk_done, 2 * n + 2)
                        for c in range(2):
                            sp.dma_start(q[c * HD:(c + 1) * HD, t % 2, c, :],
                                         qT[ds(pair * P + c * HD, HD), (q0 + t) * P:(q0 + t + 1) * P]).then_inc(q_in[t % 2], 16)
                units(sp, step)
                for u in range(2):
                    sp.wait_ge(o_out[u], 16 * (1 + pairs * nq // 2))

            @block.gpsimd
            def _(pool):
                nc.gpsimd.memset(q[:, :, :, :], 0.0).then_inc(q_zero, 1)

            @block.tensor
            def _(pe):
                pe.wait_ge(const_in, 16 * (5 if diff else 1))
                pe.sem_inc(qk_done, 4)
                pe.sem_inc(tr_done, TR0)

                def step(n, t, pair, late, scores):
                    m = n - LAG
                    slot = (t - LAG) % RING
                    for g, (c, b) in enumerate(groups):
                        if late is not None:
                            if diff:
                                pe.wait_ge(pc_done, m + 1)
                            else:
                                pe.wait_ge(p_done, 2 * m + c + 1)
                            for i, kt in enumerate(blocks[b]):
                                x = nc.tensor.transpose(tr[:, i * P:(i + 1) * P], p[:, slot, c, kt * P:(kt + 1) * P], ident[:, :])
                            x.then_inc(tr_done, 1)
                        if scores:
                            for cc, i in per_group[g]:
                                if i == 0:
                                    pe.wait_ge(q_in[t % 2], 32 * ((n - t) // 2 + t // 2 + 1))
                                    if not (isinstance(n, int) and n == 0):
                                        pe.wait_ge(p_done, 2 * n - 2 + cc + 1)
                                a, w = chunks[i]
                                x = nc.tensor.matmul(S[cc][:, a:a + w], q[:, t % 2, cc, :], K[:, kmap(pair), a:a + w], start=True, stop=True)
                                if i == len(chunks) - 1:
                                    x.then_inc(qk_done, 1)
                        if late is not None:
                            if by_act[g]:
                                pe.wait_ge(ev_act, GA * m + sum(by_act[:g]) + 1)
                            else:
                                pe.wait_ge(ev_dve, GD * m + g - sum(by_act[:g]) + 1)
                            if g == 0:
                                pe.wait_ge(o_done, m + 1)
                            for i, kt in enumerate(blocks[b]):
                                vc = late * P if diff else kmap(late) * HD
                                x = nc.tensor.matmul(acc[:, c * HD:c * HD + VW], pT[:, g, i * P:(i + 1) * P], V[:, kt, ds(vc, VW)],
                                                     start=kt == 0, stop=kt == nk - 1)
                            if g == G - 1:
                                x.then_inc(pv_done, 1)
                units(pe, step)

            def copy_out(eng, copy, sem, act, g, m):
                eng.wait_ge(tr_done, TR0 + G * m + g + 1)
                w = len(blocks[groups[g][1]]) * P
                copy(pT[:, g, 0:w], tr[:, 0:w]).then_inc(sem, 1)

            @block.vector
            def _(dve):
                if diff:
                    dve.wait_ge(const_in, 16 * 5)
                    st = Steps(lam_step)
                    for i in range(2):
                        dve.wait_ge(lam_step, st.did(nc.vector.tensor_tensor(lqk[:, 2 * i, :], lqk[:, 2 * i, :], lqk[:, 2 * i + 1, :], ALU.mult)))
                        at = st.did(nc.vector.reduce_sum(lam[:, i:i + 1], lqk[:, 2 * i, :], AX.X))
                    dve.wait_ge(lam_step, at)
                    dve.sem_inc(lam_done, 1)
                    dve.wait_ge(lam_exp, 1)
                    dve.wait_ge(lam_step, st.did(nc.vector.tensor_tensor(lam[:, 5:6], lam[:, 3:4], lam[:, 2:3], ALU.subtract)))
                    dve.wait_ge(lam_step, st.did(nc.vector.tensor_scalar(lam[:, 6:7], lam[:, 5:6], LAMBDA_INIT, None, ALU.subtract)))

                dve.sem_inc(o_done, 1)

                def maximum(n, t, c):
                    dve.wait_ge(qk_done, 4 + 2 * n + c + 1)
                    nc.vector.tensor_reduce(nmax[:, t % RING, c:c + 1], S[c][:, 0:W], AX.X, ALU.max, negate=True).then_inc(nmax_done, 1)

                def combine(n, t):
                    u = t % RING
                    st = Steps(small, 2 * n)
                    dve.wait_ge(p_done, 2 * n + 2)
                    at = st.did(nc.vector.reciprocal(recip[:, u, :], total[:, u, :]))
                    dve.wait_ge(small, at)
                    at = st.did(nc.vector.scalar_tensor_tensor(out=mix[:, u:u + 1], in0=total[:, u, 0:1], scalar=lam[:, 6:7],
                                                               in1=recip[:, u, 1:2], op0=ALU.mult, op1=ALU.mult))
                    dve.wait_ge(small, at)
                    nc.vector.scalar_tensor_tensor(out=p[:, u, 0, :], in0=p[:, u, 1, :], scalar=mix[:, u:u + 1], in1=p[:, u, 0, :],
                                                   op0=ALU.mult, op1=ALU.add).then_inc(pc_done, 1)

                def step(n, t, pair, late, scores):
                    m = n - LAG
                    mine = [g for g in range(G) if not by_act[g]]
                    if late is not None:
                        for g in mine[:-1]:
                            copy_out(dve, nc.vector.tensor_copy, ev_dve, False, g, m)
                    if scores:
                        maximum(n, t, 0)
                    if late is not None and mine:
                        copy_out(dve, nc.vector.tensor_copy, ev_dve, False, mine[-1], m)
                    if scores:
                        maximum(n, t, 1)
                        if diff:
                            combine(n, t)
                    if late is not None and not diff:
                        dve.wait_ge(p_done, 2 * m + 2)
                        nc.vector.reciprocal(recip[:, (t - LAG) % RING, :], total[:, (t - LAG) % RING, :]).then_inc(r_done, 1)
                units(dve, step)

            @block.scalar
            def _(act):
                for u in range(2):
                    act.sem_inc(o_out[u], 16)
                if diff:
                    act.wait_ge(lam_done, 1)
                    nc.scalar.activation(lam[:, 2:4], lam[:, 0:2], ACT.Exp).then_inc(lam_exp, 1)

                def exponent(n, t, c):
                    u = t % RING
                    act.wait_ge(nmax_done, 2 * n + c + 1)
                    act.wait_ge(tr_done, G * (n + 1))
                    nc.scalar.activation(p[:, u, c, :], S[c][:, 0:W], ACT.Exp, bias=nmax[:, u, c:c + 1], accum_out=total[:, u, c:c + 1]).then_inc(p_done, 1)

                def output(m, t, late):
                    u, v = t % RING, t % 2
                    act.wait_ge(pv_done, m + 1)
                    act.wait_ge(o_out[v], 16 * ((m - t) // 2 + t // 2 + 1))
                    if diff:
                        nc.scalar.activation(o[:, v, :], acc[:, 0:P], ACT.Copy, scale=recip[:, u, 0:1]).then_inc(o_done, 1)
                    else:
                        act.wait_ge(r_done, m + 1)
                        nc.scalar.activation(o[:, v, 0:HD], acc[:, 0:HD], ACT.Copy, scale=recip[:, u, 0:1])
                        nc.scalar.activation(o[:, v, HD:P], acc[:, HD:P], ACT.Copy, scale=recip[:, u, 1:2]).then_inc(o_done, 1)
                    act.wait_ge(o_done, 1 + m + 1)
                    act.dma_start(out[(q0 + t) * P:(q0 + t + 1) * P, ds(late * P, P)], o[:, v, :]).then_inc(o_out[v], 16)

                def step(n, t, pair, late, scores):
                    m = n - LAG
                    mine = [g for g in range(G) if by_act[g]]
                    if late is not None:
                        for g in mine[:-1]:
                            copy_out(act, lambda a, b: nc.scalar.activation(a, b, ACT.Copy), ev_act, True, g, m)
                    if scores:
                        exponent(n, t, 0)
                    if late is not None:
                        copy_out(act, lambda a, b: nc.scalar.activation(a, b, ACT.Copy), ev_act, True, mine[-1], m)
                    if scores:
                        exponent(n, t, 1)
                    if late is not None:
                        output(m, (t - LAG) % nq, late)
                units(act, step)


CK = 64
NCK = TOK // CK
CTXCK = CTX // CK
GAP = TOK + 1
GCH = ((0, 512), (512, 512), (1024, GAP - 1024))
DIRS = (0, 1)


def gap(t0):
    return t0 + (0 if t0 < CTX else 1)


class Plan:

    def __init__(self, sem, names):
        self.sem, self.names, self.n = sem, names, 0

    def did(self, name, ins):
        assert self.names[self.n] == name, (self.names[self.n], name)
        self.n += 1
        ins.then_inc(self.sem, 1)

    def wait(self, eng, name):
        eng.wait_ge(self.sem, self.names.index(name) + 1)


def shift(nc, dve, plan, tag, x, o, mu):
    plan.did(tag + "0", nc.vector.tensor_tensor(mu[:, 2:3], mu[:, 0:1], mu[:, 1:2], ALU.add))
    plan.wait(dve, tag + "0")
    plan.did(tag + "1", nc.vector.tensor_scalar(mu[:, 2:3], mu[:, 2:3], -1.0, 1.0, ALU.mult, ALU.add))
    plan.wait(dve, tag + "1")
    plan.did(tag + "2", nc.vector.tensor_scalar(o, x[:, 1:1 + GAP], mu[:, 2:3], None, ALU.mult))
    plan.wait(dve, tag + "2")
    plan.did(tag + "3", nc.vector.scalar_tensor_tensor(out=o, in0=x[:, 0:GAP], scalar=mu[:, 0:1], in1=o, op0=ALU.mult, op1=ALU.add))
    plan.wait(dve, tag + "3")
    plan.did(tag, nc.vector.scalar_tensor_tensor(out=o, in0=x[:, 2:2 + GAP], scalar=mu[:, 1:2], in1=o, op0=ALU.mult, op1=ALU.add))


SHIFT_STEPS = ("0", "1", "2", "3", "")


def load_padded(sp, x, rows, sem):
    sp.dma_start(x[:, 1:1 + CTX], rows[:, 0:CTX]).then_inc(sem, 16)
    sp.dma_start(x[:, CTX + 2:GAP + 1], rows[:, CTX:TOK]).then_inc(sem, 16)


def one_column(ap):
    return ap.rearrange("(p o) -> p o", o=1)


def rwkv_shared_phase(nc, sems, d, projT, lora, gate):
    with ExitStack() as ctx:
        s = Scope(nc, ctx, sems, "rsh")
        x = s.sb("x", [P, 2, GAP + 2])
        o = s.sb("o", [P, 2, GAP])
        mu = s.sb("mu", [P, 2, 3])
        zeroed, x_in, mu_in, out_done = (s.sem(n) for n in ("zeroed", "x_in", "mu_in", "out_done"))
        dv = Plan(s.sem("dve"), [f"{t}{i}" for t in ("lora", "gate") for i in SHIFT_STEPS])
        base = 3 * BW
        with nc.Block() as block:
            @block.gpsimd
            def _(pool):
                nc.gpsimd.memset(x[:, :, :], 0.0).then_inc(zeroed, 1)

            @block.sync
            def _(sp):
                sp.wait_ge(zeroed, 1)
                for u in range(2):
                    for m, name in enumerate(("ev_mu_prev", "ev_mu_next")):
                        sp.dma_start(mu[:, u, m:m + 1], one_column(d[name][0, base + u * P:base + (u + 1) * P])).then_inc(mu_in, 16)
                    load_padded(sp, x[:, u, :], projT[A_COLS + base + u * P:A_COLS + base + (u + 1) * P, :], x_in)

            @block.vector
            def _(dve):
                dve.wait_ge(mu_in, 64)
                dve.wait_ge(x_in, 64)
                shift(nc, dve, dv, "lora", x[:, 0, :], o[:, 0, :], mu[:, 0, :])
                shift(nc, dve, dv, "gate", x[:, 1, :], o[:, 1, :], mu[:, 1, :])

            @block.scalar
            def _(act):
                dv.wait(act, "lora")
                nc.scalar.activation(lora[0:HD, :], o[0:HD, 0, :], ACT.Tanh).then_inc(out_done, 1)
                nc.scalar.activation(lora[HD:P, :], o[HD:P, 0, :], ACT.Copy).then_inc(out_done, 1)
                dv.wait(act, "gate")
                nc.scalar.activation(gate[:, :], o[:, 1, :], ACT.Sigmoid).then_inc(out_done, 1)
                act.wait_ge(out_done, 3)


def rwkv_prep_phase(nc, sems, j, d, projT, lora, kr, bk, last, vflip, vtok, srk):
    with ExitStack() as ctx:
        s = Scope(nc, ctx, sems, f"rp{j}")
        x = s.sb("x", [P, 3, GAP + 2])
        o = s.sb("o", [P, 3, GAP])
        r, k, v = o[:, 0, :], o[:, 1, :], o[:, 2, :]
        mu = s.sb("mu", [P, 3, 3])
        col = s.sb("col", [P, 8])
        ones, ident = s.sb("ones", [P, P]), s.sb("ident", [P, P])
        ind = s.sb("ind", [P, 2])
        wl = s.sb("wl", [P, 4, P])
        restart = s.sb("restart", [P, 2, GAP])
        kk, nrm = s.sb("kk", [P, GAP]), s.sb("nrm", [P, GAP])
        sg, a, cum = s.sb("sg", [P, 2, GAP]), s.sb("a", [P, 2, GAP]), s.sb("cum", [P, 2, GAP])
        ex = s.sb("ex", [P, 3, GAP])
        kd, be = s.sb("kd", [P, 2, GAP]), s.sb("be", [P, GAP])
        eps = s.sb("eps", [P, 1])
        bank = [s.ps(f"bank{i}") for i in range(8)]
        zeroed, x_in, c_in, v_out = (s.sem(n) for n in ("zeroed", "x_in", "c_in", "v_out"))
        K_K, K_A, R_K, W0, A0, ONE_KA = 0, 1, 2, 3, 5, 7
        parts = [(dr, which) for which in range(2) for dr in DIRS]
        dv = Plan(s.sem("dve"), [f"{t}{i}" for t in "vkr" for i in SHIFT_STEPS] + ["one_ka", "cum0", "df0", "cum1", "df1", "nmax", "rn", "kk"]
                  + [f"{n}{dr}" for dr in DIRS for n in ("f", "kd", "be", "kap", "rho", "last", "bet", "key")] + ["ksum", "rk0", "rk"])
        ac = Plan(s.sem("act"), ["vt0", "vt1", "vt2", "sq"] + [f"{'za'[w]}{dr}{c}" for dr, w in parts for c in range(3)]
                  + ["n0", "n1", "n2"] + [f"{n}{dr}" for dr in DIRS for n in ("pex", "pin", "inv")] + ["srk"])
        pp = Plan(s.sem("pe"), ["vt0", "vt1", "vt2", "n0", "n1", "n2"] + [f"{'za'[w]}{dr}{c}" for dr, w in parts for c in range(3)] + ["srk"])
        with nc.Block() as block:
            @block.gpsimd
            def _(pool):
                nc.gpsimd.memset(x[:, :, :], 0.0).then_inc(zeroed, 1)
                nc.gpsimd.memset(wl[:, :, :], 0.0).then_inc(zeroed, 1)
                nc.gpsimd.memset(restart[:, :, :], 1.0).then_inc(zeroed, 1)
                pool.wait_ge(zeroed, 3)
                for a0, n in ((0, CTXCK), (CTX + 1, NCK - CTXCK)):
                    for dr in DIRS:
                        cks = restart[:, dr, a0:a0 + n * CK].rearrange("p (c t) -> p c t", t=CK)
                        e = dr * (CK - 1)
                        nc.gpsimd.memset(cks[:, :, e:e + 1], 0.0).then_inc(zeroed, 1)
                nc.gpsimd.memset(eps[:, :], 0.0).then_inc(zeroed, 1)

            @block.sync
            def _(sp):
                sp.wait_ge(zeroed, 2)
                for i in (2, 1, 0):
                    c0 = i * BW + j * P
                    for m, name in enumerate(("ev_mu_prev", "ev_mu_next")):
                        sp.dma_start(mu[:, i, m:m + 1], one_column(d[name][0, c0:c0 + P])).then_inc(x_in, 16)
                    load_padded(sp, x[:, i, :], projT[A_COLS + c0:A_COLS + c0 + P, :], x_in)
                hs = slice(j * P, (j + 1) * P)
                cols = [(K_K, d["ev_k_k"][0, hs]), (K_A, d["ev_k_a"][0, hs]), (R_K, d["ev_r_k"][0, 2 * j:2 * j + 2].rearrange("h c -> (h c)"))]
                cols += [(W0 + dr, d["ev_w0"][0, dr, hs]) for dr in DIRS] + [(A0 + dr, d["ev_a0"][0, dr, hs]) for dr in DIRS]
                for c, src in cols:
                    sp.dma_start(col[:, c:c + 1], one_column(src)).then_inc(c_in, 16)
                for dr in DIRS:
                    sp.dma_start(wl[0:HD, dr, :], d["ev_w2"][0, dr, :, hs]).then_inc(c_in, 16)
                    sp.dma_start(wl[HD:P, 2 + dr, :], d["ev_a2"][0, dr, :, hs]).then_inc(c_in, 16)
                sp.dma_start(ones[:, :], d["headones"]).then_inc(c_in, 16)
                sp.dma_start(ident[:, :], d["ident"]).then_inc(c_in, 16)
                sp.dma_start(ind[:, :], d["headcols"]).then_inc(c_in, 16)
                ac.wait(sp, "vt2")
                for half in range(2):
                    for h in range(2):
                        sp.dma_start(vflip[(1 - h) * HD:(2 - h) * HD, half:NCK:2, :],
                                     vtok[half * HD:(half + 1) * HD, :, j * P + h * HD:j * P + (h + 1) * HD]).then_inc(v_out, 16)
                sp.wait_ge(v_out, 64)

            C_IN = 16 * 14

            @block.tensor
            def _(pe):
                pe.wait_ge(c_in, C_IN)
                dv.wait(pe, "v")
                for b in range(3):
                    for t in range(4 * b, min(4 * b + 4, NT)):
                        mm = nc.tensor.transpose(bank[b][:, (t - 4 * b) * P:(t - 4 * b + 1) * P], v[:, gap(t * P):gap(t * P) + P], ident[:, :])
                    pp.did(f"vt{b}", mm)
                ac.wait(pe, "sq")
                for c, (t0, w) in enumerate(GCH):
                    pp.did(f"n{c}", nc.tensor.matmul(bank[3 + c][:, 0:w], ones[:, :], nrm[:, t0:t0 + w], start=True, stop=True))
                for n, (dr, which) in enumerate(parts):
                    for c, (t0, w) in enumerate(GCH):
                        q = 3 * n + c
                        if q < 2:
                            ac.wait(pe, f"vt{q}")
                        else:
                            pn, pc = divmod(q - 2, 3)
                            ac.wait(pe, f"{'za'[parts[pn][1]]}{parts[pn][0]}{pc}")
                        pp.did(f"{'za'[which]}{dr}{c}", nc.tensor.matmul(bank[q % 2][:, 0:w], wl[:, 2 * which + dr, :], lora[:, t0:t0 + w], start=True, stop=True))
                dv.wait(pe, "rk")
                for t in range(NT):
                    mm = nc.tensor.matmul(bank[2][:, 2 * t:2 * t + 2], be[:, gap(t * P):gap(t * P) + P], ind[:, :], start=True, stop=True)
                pp.did("srk", mm)

            @block.scalar
            def _(act):
                for b in range(3):
                    pp.wait(act, f"vt{b}")
                    w = min(4, NT - 4 * b)
                    ac.did(f"vt{b}", nc.scalar.activation(vtok[:, 4 * b:4 * b + w, j * P:(j + 1) * P], bank[b][:, 0:w * P].rearrange("p (t c) -> p t c", c=P), ACT.Copy))
                act.wait_ge(c_in, C_IN)
                act.wait_ge(zeroed, 8)
                dv.wait(act, "k")
                ac.did("sq", nc.scalar.activation(nrm[:, :], k, ACT.Square, scale=col[:, K_K:K_K + 1]))
                for dr, which in parts:
                    for c, (t0, w) in enumerate(GCH):
                        name = f"{'za'[which]}{dr}{c}"
                        pp.wait(act, name)
                        q = 3 * parts.index((dr, which)) + c
                        to, c0 = (sg, W0) if which == 0 else (a, A0)
                        ac.did(name, nc.scalar.activation(to[:, dr, t0:t0 + w], bank[q % 2][:, 0:w], ACT.Sigmoid, bias=col[:, c0 + dr:c0 + dr + 1]))
                pp.wait(act, "n2")
                for c, (t0, w) in enumerate(GCH):
                    ac.did(f"n{c}", nc.scalar.activation(nrm[:, t0:t0 + w], bank[3 + c][:, 0:w], ACT.Sqrt))
                for dr in DIRS:
                    dv.wait(act, f"df{dr}")
                    if dr:
                        dv.wait(act, "kap0")
                    ac.did(f"pex{dr}", nc.scalar.activation(ex[:, 0, :], sg[:, dr, :], ACT.Exp, scale=-DECAY))
                    if dr:
                        dv.wait(act, "last0")
                    ac.did(f"pin{dr}", nc.scalar.activation(ex[:, 1, :], cum[:, dr, :], ACT.Exp, scale=-DECAY))
                    if dr:
                        dv.wait(act, "key0")
                    ac.did(f"inv{dr}", nc.scalar.activation(ex[:, 2, :], cum[:, dr, :], ACT.Exp, scale=DECAY))
                pp.wait(act, "srk")
                ac.did("srk", nc.scalar.activation(srk[:, :, 2 * j:2 * j + 2], bank[2][:, 0:2 * NT].rearrange("p (t h) -> p t h", h=2), ACT.Copy))
                ac.wait(act, "srk")

            @block.vector
            def _(dve):
                dve.wait_ge(x_in, 16 * 12)
                for i, t in ((2, "v"), (1, "k"), (0, "r")):
                    shift(nc, dve, dv, t, x[:, i, :], o[:, i, :], mu[:, i, :])
                dve.wait_ge(c_in, C_IN)
                dve.wait_ge(zeroed, 8)
                dv.did("one_ka", nc.vector.tensor_scalar(col[:, ONE_KA:ONE_KA + 1], col[:, K_A:K_A + 1], -1.0, 1.0, ALU.mult, ALU.add))
                for dr in DIRS:
                    ac.wait(dve, f"z{dr}2")
                    way = slice(None, None, -1) if dr else slice(None)
                    dv.did(f"cum{dr}", nc.vector.tensor_tensor_scan(cum[:, dr, way], restart[:, dr, way], sg[:, dr, way], 0.0, ALU.mult, ALU.add))
                    dv.wait(dve, f"cum{dr}")
                    dv.did(f"df{dr}", nc.vector.tensor_tensor(sg[:, dr, :], cum[:, dr, :], sg[:, dr, :], ALU.subtract))
                ac.wait(dve, "n2")
                dv.did("nmax", nc.vector.tensor_scalar(nrm[:, :], nrm[:, :], 1e-12, None, ALU.max))
                dv.wait(dve, "nmax")
                dv.did("rn", nc.vector.reciprocal(nrm[:, :], nrm[:, :]))
                dv.wait(dve, "rn")
                dv.did("kk", nc.vector.scalar_tensor_tensor(out=kk[:, :], in0=k, scalar=col[:, K_K:K_K + 1], in1=nrm[:, :], op0=ALU.mult, op1=ALU.mult))
                dv.wait(dve, "kk")
                for dr in DIRS:
                    ac.wait(dve, f"a{dr}2")
                    dv.did(f"f{dr}", nc.vector.tensor_scalar(nrm[:, :], a[:, dr, :], col[:, K_A:K_A + 1], col[:, ONE_KA:ONE_KA + 1], ALU.mult, ALU.add))
                    dv.wait(dve, f"f{dr}")
                    dv.did(f"kd{dr}", nc.vector.tensor_tensor(kd[:, dr, :], k, nrm[:, :], ALU.mult))
                    dv.did(f"be{dr}", nc.vector.tensor_tensor(be[:, :], kk[:, :], a[:, dr, :], ALU.mult))
                    ac.wait(dve, f"pex{dr}")
                    dv.did(f"kap{dr}", nc.vector.tensor_tensor(kr[:, dr, 0, :], kk[:, :], ex[:, 0, :], ALU.mult))
                    ac.wait(dve, f"pin{dr}")
                    dv.did(f"rho{dr}", nc.vector.tensor_tensor(kr[:, dr, 1, :], r, ex[:, 1, :], ALU.mult))
                    e = 0 if dr else CK - 1
                    nc.vector.tensor_copy(last[:, dr, 0:CTXCK], ex[:, 1, e:CTX:CK])
                    dv.did(f"last{dr}", nc.vector.tensor_copy(last[:, dr, CTXCK:NCK], ex[:, 1, CTX + 1 + e:GAP:CK]))
                    ac.wait(dve, f"inv{dr}")
                    dv.wait(dve, f"be{dr}")
                    dv.did(f"bet{dr}", nc.vector.tensor_tensor(bk[:, dr, 0, :], be[:, :], ex[:, 2, :], ALU.mult))
                    dv.did(f"key{dr}", nc.vector.tensor_tensor(bk[:, dr, 1, :], kd[:, dr, :], ex[:, 2, :], ALU.mult))
                dv.did("ksum", nc.vector.tensor_tensor(nrm[:, :], kd[:, 0, :], kd[:, 1, :], ALU.add))
                dv.wait(dve, "ksum")
                dv.did("rk0", nc.vector.tensor_scalar(nrm[:, :], nrm[:, :], col[:, R_K:R_K + 1], None, ALU.mult))
                dv.wait(dve, "rk0")
                dv.did("rk", nc.vector.tensor_tensor(be[:, :], nrm[:, :], r, ALU.mult))
                dv.wait(dve, "rk")


class Rounds:

    def __init__(self, sem, names):
        self.sem, self.names, self.n = sem, names, 0

    def did(self, name, ins):
        assert self.names[self.n % len(self.names)] == name, (self.names[self.n % len(self.names)], name)
        self.n += 1
        ins.then_inc(self.sem, 1)

    def wait(self, eng, name, m):
        eng.wait_ge(self.sem, len(self.names) * m + self.names.index(name) + 1)


LEVELS = range(1, 6)


def rwkv_scan_phase(nc, sems, j, d, kr, bk, last, vflip, yout):
    ROUNDS = NCK // 2
    CR = CTXCK // 2
    with ExitStack() as ctx:
        s = Scope(nc, ctx, sems, f"rs{j}")
        ident, levels = s.sb("ident", [P, P]), s.sb("levels", [P, 6, P])
        tri, first = s.sb("tri", [P, 2, 2, 2, P]), s.sb("first", [P, 2, 2, P])
        BK = s.sb("BK", [P, 2, 2, 2, CK])
        KR = s.sb("KR", [P, 2, 2, 2, 2, P])
        gm = s.sb("gm", [P, 2, 2, 2, 2, 2, P])
        btm = s.sb("btm", [P, 2, 2, 2, 2, P])
        Yf = s.sb("Yf", [P, 2, 2, 2, P])
        Bm = s.sb("Bm", [P, 2, 2, 6, P])
        X, Y, Z = (s.sb(n, [P, 2, 2, P]) for n in "XYZ")
        R, U, S, Sl = (s.sb(n, [P, 2, HD]) for n in ("R", "U", "S", "Sl"))
        y = s.sb("y", [P, 2, NCK, HD])
        bankY = [s.ps(f"bankY{g}") for g in range(2)]
        bankZ = [s.ps(f"bankZ{g}") for g in range(2)]
        bankS = [s.ps(f"bankS{dr}") for dr in DIRS]
        bankO = [s.ps(f"bankO{dr}") for dr in DIRS]
        c_in, zeroed, y_sum, y_out = (s.sem(n) for n in ("c_in", "zeroed", "y_sum", "y_out"))
        z_done = s.sem("z_done")
        GS = range(2)
        pg = Rounds(s.sem("pe_G"), [f"G{g}" for g in GS])
        pa = Rounds(s.sem("pe_inv"), [f"T{g}" for g in GS] + [f"X{g}" for g in GS] + [f"L{l}{x}{g}" for l in LEVELS for x in "ab" for g in GS])
        aa = Rounds(s.sem("act_inv"), [f"bt{g}" for g in GS] + [f"X{g}" for g in GS] + [f"Y{l}{g}" for l in LEVELS if l > 1 for g in GS])
        va = Rounds(s.sem("dve_inv"), [f"Y{g}" for g in GS] + [f"m{g}" for g in GS] + ["gm0", "Z10", "Z11", "gm1", "X10", "X11", "B0", "B1"]
                    + [f"{x}{l}{g}" for l in LEVELS if l > 1 for x in "ZX" for g in GS])
        ga = Rounds(s.sem("pool_inv"), [f"B{g}" for g in GS])
        gk = Rounds(s.sem("pool_bk"), [f"bk{g}" for g in GS])
        ak = Rounds(s.sem("act_kr"), [f"kr{g}" for g in GS])
        pb = Rounds(s.sem("pe_seq"), [f"{n}{c}{dr}" for c in GS for n in "RUyd" for dr in DIRS])
        ab = Rounds(s.sem("act_seq"), [f"{n}{c}{dr}" for c in GS for n in "RUy" for dr in DIRS])
        vb = Rounds(s.sem("dve_seq"), [f"S{c}{dr}" for c in GS for dr in DIRS])
        gb = Rounds(s.sem("pool_seq"), [f"Sl{c}{dr}" for c in GS for dr in DIRS])

        def chunk(m, c, dr, context):
            e = 2 * m + c
            if dr:
                e = e * -1 + ((CTXCK if context else CTXCK + NCK) - 1)
            return e, e * CK + (0 if context else 1)

        def rounds(eng, body):
            for t in range(CR + 1):
                body(t, t % 2, True, t > 0, t < CR, t - 1 < CR)
            first = CR + 1
            n = (ROUNDS - first) // 2
            with eng.Fori(0, n) as i:
                for u in range(2):
                    body(2 * i + first + u, (first + u) % 2, True, True, False, False)
            for t in range(first + 2 * n, ROUNDS + 1):
                body(t, t % 2, t < ROUNDS, True, False, False)

        with nc.Block() as block:
            @block.sync
            def _(sp):
                for t, n in ((ident, "ident"), (levels, "levels"), (tri, "tri"), (first, "first")):
                    sp.dma_start(t[:], d[n]).then_inc(c_in, 16)
                sp.wait_ge(y_sum, 1)
                for h in range(2):
                    sp.dma_start(yout[:, (2 * j + h) * HD:(2 * j + h + 1) * HD].rearrange("(e t) v -> t e v", t=CK), y[h * CK:(h + 1) * CK, 0, :, :]).then_inc(y_out, 16)
                sp.wait_ge(y_out, 32)

            @block.gpsimd
            def _(pool):
                nc.gpsimd.memset(KR[:, :, :, :, :, :], 0.0).then_inc(zeroed, 1)
                nc.gpsimd.memset(S[:, :, :], 0.0).then_inc(zeroed, 1)
                nc.gpsimd.memset(btm[:, :, :, :, :, :], 0.0).then_inc(zeroed, 1)
                pool.wait_ge(zeroed, 3)
                pool.wait_ge(c_in, 64)

                def stage(m, g, context):
                    for dr in DIRS:
                        _e, c0 = chunk(m, g, dr, context)
                        nc.gpsimd.tensor_copy(BK[0:HD, g, dr, :, :], bk[0:HD, dr, :, ds(c0, CK)])
                        nc.gpsimd.tensor_copy(BK[HD:P, g, dr, 1, :], bk[HD:P, dr, 0, ds(c0, CK)])
                        x = nc.gpsimd.tensor_copy(BK[HD:P, g, dr, 0, :], bk[HD:P, dr, 1, ds(c0, CK)])
                    gk.did(f"bk{g}", x)

                def body(m, par, inv, seq, ctx_inv, ctx_seq):
                    if inv:
                        gk.wait(pool, "bk1", m)
                    for c in GS:
                        if seq:
                            for dr in DIRS:
                                if c:
                                    vb.wait(pool, f"S0{dr}", m - 1)
                                elif not (isinstance(m, int) and m == 1):
                                    vb.wait(pool, f"S1{dr}", m - 2)
                                e, _c0 = chunk(m - 1, c, dr, ctx_seq)
                                gb.did(f"Sl{c}{dr}", nc.gpsimd.tensor_tensor(Sl[:, dr, :], S[:, dr, :], last[:, dr, ds(e, 1)].to_broadcast([P, HD]), ALU.mult))
                        if inv and c == 0:
                            for g in GS:
                                va.wait(pool, f"gm{g}", m)
                                for dr in DIRS:
                                    x = nc.gpsimd.tensor_tensor(Bm[:, g, dr, 3:6, :], gm[:, par, g, dr, 0, 0:1, :].to_broadcast([P, 3, P]), levels[:, 3:6, :], ALU.mult)
                                ga.did(f"B{g}", x)
                            if not (isinstance(m, int) and m == ROUNDS - 1):
                                ga.wait(pool, "B1", m)
                                for g in GS:
                                    pa.wait(pool, f"T{g}", m)
                                    stage(m + 1, g, ctx_inv and not (isinstance(m, int) and m + 1 >= CR))
                                gk.wait(pool, "bk1", m + 1)
                for g in GS:
                    stage(0, g, True)
                rounds(pool, body)

            @block.tensor
            def _(pe):
                pe.wait_ge(c_in, 64)

                def body(m, par, inv, seq, ctx_inv, ctx_seq):
                    q = 1 - par

                    def right(c):
                        for dr in DIRS:
                            if c:
                                vb.wait(pe, f"S0{dr}", m - 1)
                            elif not (isinstance(m, int) and m == 1):
                                vb.wait(pe, f"S1{dr}", m - 2)
                            e, _c0 = chunk(m - 1, c, dr, ctx_seq)
                            if c == 0:
                                va.wait(pe, "X51", m - 1)
                            nc.tensor.matmul(bankS[dr][:, 0:HD], KR[:, q, c, dr, 0, :], S[:, dr, :], start=True, stop=False)
                            pb.did(f"R{c}{dr}", nc.tensor.matmul(bankS[dr][:, 0:HD], gm[:, q, c, dr, 0, 1, :], vflip[:, ds(e, 1), :], start=False, stop=True))

                    def solve(c):
                        for dr in DIRS:
                            ab.wait(pe, f"R{c}{dr}", m - 1)
                            pb.did(f"U{c}{dr}", nc.tensor.matmul(bankS[dr][:, HD:2 * HD], Yf[:, q, c, dr, :], R[:, dr, :], start=True, stop=True))

                    def outputs(c):
                        for dr in DIRS:
                            e, _c0 = chunk(m - 1, c, dr, ctx_seq)
                            if c:
                                ab.wait(pe, f"y0{dr}", m - 1)
                            elif not (isinstance(m, int) and m == 1):
                                ab.wait(pe, f"y1{dr}", m - 2)
                            ab.wait(pe, f"U{c}{dr}", m - 1)
                            vf = vflip[:, ds(e, 1), :]
                            nc.tensor.matmul(bankO[dr][:, 0:HD], KR[:, q, c, dr, 1, :], S[:, dr, :], start=True, stop=False)
                            nc.tensor.matmul(bankO[dr][:, 0:HD], gm[:, q, c, dr, 1, 1, :], vf, start=False, stop=False)
                            pb.did(f"y{c}{dr}", nc.tensor.matmul(bankO[dr][:, 0:HD], gm[:, q, c, dr, 1, 0, :], U[:, dr, :], start=False, stop=True))
                        for dr in DIRS:
                            e, _c0 = chunk(m - 1, c, dr, ctx_seq)
                            nc.tensor.matmul(bankS[dr][:, 2 * HD:3 * HD], btm[:, q, c, dr, 1, :], vflip[:, ds(e, 1), :], start=True, stop=False)
                            pb.did(f"d{c}{dr}", nc.tensor.matmul(bankS[dr][:, 2 * HD:3 * HD], btm[:, q, c, dr, 0, :], U[:, dr, :], start=False, stop=True))

                    def turn_rows():
                        for g in GS:
                            if not (isinstance(m, int) and m == 0):
                                va.wait(pe, f"X5{g}", m - 1)
                            for dr in DIRS:
                                x = nc.tensor.transpose(bankY[g][:, dr * P:(dr + 1) * P], BK[:, g, dr, :, :].rearrange("p a t -> p (a t)"), ident[:, :])
                            pa.did(f"T{g}", x)

                    def first_inverse():
                        for g in GS:
                            va.wait(pe, f"Y{g}", m)
                            aa.wait(pe, f"bt{g}", m)
                            for dr in DIRS:
                                x = nc.tensor.transpose(bankY[g][:, dr * P:(dr + 1) * P], Y[:, g, dr, :], ident[:, :])
                            pa.did(f"X{g}", x)

                    def level_a(l):
                        for g in GS:
                            if l == 1:
                                aa.wait(pe, f"X{g}", m)
                                va.wait(pe, f"m{g}", m)
                            else:
                                va.wait(pe, f"B{g}" if l == 2 else f"X{l - 1}{g}", m)
                                if l == 3:
                                    ga.wait(pe, f"B{g}", m)
                            for dr in DIRS:
                                if l > 1:
                                    nc.tensor.transpose(bankY[g][:, dr * P:(dr + 1) * P], X[:, g, dr, :], ident[:, :])
                                to = bankY[g][:, 256 + dr * P:256 + (dr + 1) * P] if l == 1 else bankZ[g][:, dr * P:(dr + 1) * P]
                                x = nc.tensor.matmul(to, Bm[:, g, dr, l, :], X[:, g, dr, :], start=True, stop=True)
                            pa.did(f"L{l}a{g}", x)

                    def level_b(l):
                        for g in GS:
                            va.wait(pe, f"Z{l}{g}", m)
                            if l > 1:
                                aa.wait(pe, f"Y{l}{g}", m)
                            for dr in DIRS:
                                a, b = (Z, Y) if l == 5 else (Y, Z)
                                x = nc.tensor.matmul(bankY[g][:, 256 + dr * P:256 + (dr + 1) * P], a[:, g, dr, :], b[:, g, dr, :], start=True, stop=True)
                            pa.did(f"L{l}b{g}", x)

                    if inv:
                        turn_rows()
                    if seq:
                        right(0)
                    if inv:
                        first_inverse()
                    if seq:
                        solve(0)
                    if inv:
                        level_a(1)
                    if seq:
                        outputs(0)
                    if inv:
                        level_b(1)
                        level_a(2)
                    if seq:
                        right(1)
                    if inv:
                        level_b(2)
                        level_a(3)
                    if seq:
                        solve(1)
                    if inv:
                        level_b(3)
                        level_a(4)
                    if seq:
                        outputs(1)
                    if inv:
                        level_b(4)
                        level_a(5)
                        if not (isinstance(m, int) and m == ROUNDS - 1):
                            products(m + 1, 1 - par)
                        level_b(5)

                def products(m, par):
                    for g in GS:
                        gk.wait(pe, f"bk{g}", m)
                        ak.wait(pe, f"kr{g}", m)
                        if not (isinstance(m, int) and m == 0):
                            va.wait(pe, f"Z5{g}", m - 1)
                        for dr in DIRS:
                            x = nc.tensor.matmul(bankZ[g][:, dr * 256:(dr + 1) * 256], BK[:, g, dr, :, :].rearrange("p a t -> p (a t)"), KR[:, par, g, dr, :, :], start=True, stop=True)
                        pg.did(f"G{g}", x)
                products(0, 0)
                rounds(pe, body)

            @block.scalar
            def _(act):
                act.wait_ge(zeroed, 3)

                def stage(m, par, g, context):
                    for dr in DIRS:
                        _e, c0 = chunk(m, g, dr, context)
                        for h in range(2):
                            hp = slice(h * HD, (h + 1) * HD)
                            x = nc.scalar.activation(KR[hp, par, g, dr, :, h * CK:(h + 1) * CK], kr[hp, dr, :, ds(c0, CK)], ACT.Copy)
                    ak.did(f"kr{g}", x)

                def stage_next(m, par, g, ctx_inv, seq):
                    if not (isinstance(m, int) and m >= ROUNDS - 1):
                        if seq:
                            pb.wait(act, f"d{g}1", m - 1)
                        stage(m + 1, 1 - par, g, ctx_inv and not (isinstance(m, int) and m + 1 >= CR))

                def body(m, par, inv, seq, ctx_inv, ctx_seq):
                    def copies(c, name):
                        for dr in DIRS:
                            pb.wait(act, f"{name}{c}{dr}", m - 1)
                            if name == "y":
                                e, _c0 = chunk(m - 1, c, dr, ctx_seq)
                                ab.did(f"y{c}{dr}", nc.scalar.activation(y[:, dr, ds(e, 1), :], bankO[dr][:, 0:HD].rearrange("p (o v) -> p o v", o=1), ACT.Copy))
                            else:
                                to, c0 = (R, 0) if name == "R" else (U, HD)
                                ab.did(f"{name}{c}{dr}", nc.scalar.activation(to[:, dr, :], bankS[dr][:, c0:c0 + HD], ACT.Copy))

                    def inverse(l):
                        for g in GS:
                            pa.wait(act, f"X{g}" if l == 1 else f"L{l}a{g}", m)
                            to = X if l == 1 else Y
                            aa.did(f"X{g}" if l == 1 else f"Y{l}{g}", nc.scalar.activation(to[:, g, :, :], bankY[g][:, 0:256].rearrange("p (d t) -> p d t", d=2), ACT.Copy))

                    def turned():
                        if not (isinstance(m, int) and m < 2):
                            pb.wait(act, "d11", m - 2)
                        for g in GS:
                            pa.wait(act, f"T{g}", m)
                            T = bankY[g][:, 0:256].rearrange("p (d t) -> p d t", d=2)
                            for h in range(2):
                                hp, other = slice(h * HD, (h + 1) * HD), slice((1 - h) * HD, (2 - h) * HD)
                                nc.scalar.activation(btm[hp, par, g, :, 0, hp], T[hp, :, hp], ACT.Copy, scale=-1.0)
                                x = nc.scalar.activation(btm[hp, par, g, :, 1, other], T[hp, :, other], ACT.Copy)
                            aa.did(f"bt{g}", x)

                    if inv:
                        turned()
                    if seq:
                        copies(0, "R")
                    if inv:
                        inverse(1)
                    if seq:
                        copies(0, "U")
                        copies(0, "y")
                    if inv:
                        inverse(2)
                    if seq:
                        copies(1, "R")
                    if inv:
                        inverse(3)
                    if seq:
                        copies(1, "U")
                    if inv:
                        inverse(4)
                        stage_next(m, par, 0, ctx_inv, seq)
                    if seq:
                        copies(1, "y")
                    if inv:
                        stage_next(m, par, 1, ctx_inv, seq)
                        inverse(5)
                for g in GS:
                    stage(0, 0, g, True)
                rounds(act, body)
                ab.wait(act, "y11", ROUNDS - 1)

            @block.vector
            def _(dve):
                dve.wait_ge(c_in, 64)
                dve.wait_ge(zeroed, 2)

                def body(m, par, inv, seq, ctx_inv, ctx_seq):
                    def state(c):
                        for dr in DIRS:
                            e, _c0 = chunk(m - 1, c, dr, ctx_seq)
                            gb.wait(dve, f"Sl{c}{dr}", m - 1)
                            pb.wait(dve, f"d{c}{dr}", m - 1)
                            vb.did(f"S{c}{dr}", nc.vector.scalar_tensor_tensor(out=S[:, dr, :], in0=bankS[dr][:, 2 * HD:3 * HD], scalar=last[:, dr, ds(e, 1)],
                                                                               in1=Sl[:, dr, :], op0=ALU.mult, op1=ALU.add))

                    def masks():
                        for g in GS:
                            pg.wait(dve, f"G{g}", m)
                            nc.vector.tensor_tensor(Z[:, g, :, :], bankZ[g][:, :].rearrange("p (d k t) -> p d k t", d=2, k=2)[:, :, 0, :], first[:, 0, :, :], ALU.mult).then_inc(z_done, 1)
                            dve.wait_ge(z_done, 2 * m + g + 1)
                            va.did(f"Y{g}", nc.vector.tensor_tensor(Y[:, g, :, :], ident[:, :].rearrange("p (o t) -> p o t", o=1).to_broadcast([P, 2, P]), Z[:, g, :, :], ALU.add))
                        for g in GS:
                            va.did(f"m{g}", nc.vector.tensor_tensor(Bm[:, g, :, 1, :], bankZ[g][:, :].rearrange("p (d k t) -> p d k t", d=2, k=2)[:, :, 0, :], first[:, 1, :, :], ALU.mult))
                        if not (isinstance(m, int) and m < 2):
                            pb.wait(dve, "d11", m - 2)

                    def masked(g):
                        pair = bankZ[g][:, :].rearrange("p (k o t) -> p k o t", o=1, t=P).to_broadcast([P, 4, 2, P])
                        va.did(f"gm{g}", nc.vector.tensor_tensor(gm[:, par, g, :, :, :, :].rearrange("p a b c t -> p (a b) c t"), pair,
                                                                 tri[:, :, :, :, :].rearrange("p a b c t -> p (a b) c t"), ALU.mult))

                    def take_product(l, g):
                        pa.wait(dve, f"L{l}a{g}", m)
                        at = bankY[g][:, 256:512] if l == 1 else bankZ[g][:, 0:256]
                        va.did(f"Z{l}{g}", nc.vector.tensor_copy(Z[:, g, :, :], at.rearrange("p (d t) -> p d t", d=2)))

                    def correct(l, g):
                        pa.wait(dve, f"L{l}b{g}", m)
                        corr = bankY[g][:, 256:512].rearrange("p (d t) -> p d t", d=2)
                        if l == 5:
                            va.did(f"X5{g}", nc.vector.tensor_tensor(Yf[:, par, g, :, :], Y[:, g, :, :], corr, ALU.subtract))
                        else:
                            va.did(f"X{l}{g}", nc.vector.tensor_tensor(X[:, g, :, :], X[:, g, :, :], corr, ALU.subtract))

                    def level(l):
                        for g in GS:
                            take_product(l, g)
                        for g in GS:
                            correct(l, g)

                    def first_level():
                        masked(0)
                        for g in GS:
                            take_product(1, g)
                        masked(1)
                        for g in GS:
                            correct(1, g)
                        for g in GS:
                            va.wait(dve, f"gm{g}", m)
                            va.did(f"B{g}", nc.vector.tensor_tensor(Bm[:, g, :, 2, :], gm[:, par, g, :, 0, 0, :], levels[:, 2:3, :].to_broadcast([P, 2, P]), ALU.mult))

                    if inv:
                        masks()
                        first_level()
                    if seq:
                        state(0)
                    if inv:
                        for l in (2, 3):
                            level(l)
                        level(4)
                    if seq:
                        state(1)
                    if inv:
                        level(5)
                rounds(dve, body)
                ab.wait(dve, "y11", ROUNDS - 1)
                nc.vector.tensor_tensor(y[:, 0, :, :], y[:, 0, :, :], y[:, 1, :, :], ALU.add).then_inc(y_sum, 1)


def row_of(ap):
    return ap.rearrange("(o n) -> o n", o=1).to_broadcast([P, ap.shape[0]])


def pair_loop(eng, first, body):
    if first < CT:
        body(0, 0, 1)
    else:
        body(first // 2, 0, 0)
    with eng.Fori(first // 2 + 1, NT // 2) as i:
        body(i, i - first // 2, 0)


def is0(m):
    return isinstance(m, int) and m == 0


def readout_phase(nc, sems, d, y, gate, vtok, srk, out):
    with ExitStack() as ctx:
        s = Scope(nc, ctx, sems, "ro")
        g2, gnw, gnb = (s.sb(n, [P, BW]) for n in ("g2", "gnw", "gnb"))
        eps = s.sb("eps", [P, 1])
        x, sq, t, bonus, o = (s.sb(n, [P, 2, BW]) for n in ("x", "sq", "t", "bonus", "o"))
        gs = s.sb("gs", [P, 2, P])
        mean, var, sd, rs = (s.sb(n, [P, 2, BH]) for n in ("mean", "var", "sd", "rs"))
        acc = [s.ps(f"acc{u}") for u in range(2)]
        c_in, eps_set = s.sem("c_in"), s.sem("eps_set")
        x_in, o_out = [s.sem(f"x_in{u}") for u in range(2)], [s.sem(f"o_out{u}") for u in range(2)]
        US = range(2)
        dv = Rounds(s.sem("dve"), [f"{n}{u}" for n in ("sum", "mean", "cen", "var", "rs", "nrm", "out") for u in US])
        ac = Rounds(s.sem("act"), [f"{n}{u}" for n in ("sq", "sd") for u in US])
        po = Rounds(s.sem("pool"), [f"gs{u}" for u in US] + [f"bonus{u}" for u in US] + [f"{n}{u}" for n in ("w", "b", "sum") for u in US])
        pp = Rounds(s.sem("pe"), [f"g{u}" for u in US])
        heads = lambda z: z.rearrange("p (h c) -> p h c", c=HD)
        spread = lambda z: z.rearrange("p (h o) -> p h o", o=1).to_broadcast([P, BH, HD])
        rounds = NT // 2

        with nc.Block() as block:
            @block.sync
            def _(sp):
                sp.dma_start(g2[:, :], d["ev_g2"][0]).then_inc(c_in, 16)
                sp.dma_start(gnw[:, :], row_of(d["ev_gn_w"][0])).then_inc(c_in, 16)
                sp.dma_start(gnb[:, :], row_of(d["ev_gn_b"][0])).then_inc(c_in, 16)

                def body(i, m, _c):
                    for u in US:
                        if not is0(m):
                            dv.wait(sp, f"cen{u}", m - 1)
                        sp.dma_start(x[:, u, :], y[ds(i * (2 * P) + u * P, P), :]).then_inc(x_in[u], 16)
                pair_loop(sp, 0, body)

            @block.gpsimd
            def _(pool):
                pool.wait_ge(c_in, 48)

                def body(i, m, cond):
                    c0 = i * (2 * P) + (0 if cond else 1)
                    for u in US:
                        if not is0(m):
                            pp.wait(pool, f"g{u}", m - 1)
                        po.did(f"gs{u}", nc.gpsimd.tensor_copy(gs[:, u, :], gate[:, ds(c0 + u * P, P)]))
                    for u in US:
                        if not is0(m):
                            po.wait(pool, f"sum{u}", m - 1)
                        po.did(f"bonus{u}", nc.gpsimd.tensor_tensor(heads(bonus[:, u, :]), vtok[:, ds(i * 2 + u, 1), :].rearrange("p o (h c) -> p (o h) c", c=HD),
                                                                    srk[:, ds(i * 2 + u, 1), :].rearrange("p o h -> p h o").to_broadcast([P, BH, HD]), ALU.mult))
                    for u in US:
                        dv.wait(pool, f"nrm{u}", m)
                        po.did(f"w{u}", nc.gpsimd.tensor_tensor(t[:, u, :], t[:, u, :], gnw[:, :], ALU.mult))
                    for u in US:
                        po.wait(pool, f"w{u}", m)
                        po.wait(pool, f"bonus{u}", m)
                        po.did(f"b{u}", nc.gpsimd.tensor_tensor(bonus[:, u, :], bonus[:, u, :], gnb[:, :], ALU.add))
                    for u in US:
                        po.wait(pool, f"b{u}", m)
                        po.did(f"sum{u}", nc.gpsimd.tensor_tensor(t[:, u, :], t[:, u, :], bonus[:, u, :], ALU.add))
                pair_loop(pool, 0, body)

            @block.tensor
            def _(pe):
                pe.wait_ge(c_in, 48)

                def body(i, m, _c):
                    for u in US:
                        po.wait(pe, f"gs{u}", m)
                        if not is0(m):
                            dv.wait(pe, f"out{u}", m - 1)
                        pp.did(f"g{u}", nc.tensor.matmul(acc[u][:, :], gs[:, u, :], g2[:, :], start=True, stop=True))
                pair_loop(pe, 0, body)

            @block.scalar
            def _(act):
                for u in US:
                    act.sem_inc(o_out[u], 16)
                act.wait_ge(eps_set, 1)

                def body(i, m, _c):
                    for u in US:
                        dv.wait(act, f"cen{u}", m)
                        ac.did(f"sq{u}", nc.scalar.activation(sq[:, u, :], t[:, u, :], ACT.Square))
                    for u in US:
                        dv.wait(act, f"var{u}", m)
                        ac.did(f"sd{u}", nc.scalar.activation(sd[:, u, :], var[:, u, :], ACT.Sqrt, scale=1.0 / HD, bias=eps[:, 0:1]))
                    for u in US:
                        dv.wait(act, f"out{u}", m)
                        act.dma_start(out[ds(i * (2 * P) + u * P, P), AW:AW + BW], o[:, u, :]).then_inc(o_out[u], 16)
                pair_loop(act, 0, body)
                for u in US:
                    act.wait_ge(o_out[u], 16 * (rounds + 1))

            @block.vector
            def _(dve):
                nc.vector.memset(eps[:, :], GN_EPS).then_inc(eps_set, 1)

                def body(i, m, _c):
                    for u in US:
                        dve.wait_ge(x_in[u], 16 * m + 16)
                        dv.did(f"sum{u}", nc.vector.reduce_sum(mean[:, u, :], heads(x[:, u, :]), AX.X))
                    for u in US:
                        dv.wait(dve, f"sum{u}", m)
                        dv.did(f"mean{u}", nc.vector.tensor_scalar(mean[:, u, :], mean[:, u, :], 1.0 / HD, None, ALU.mult))
                    for u in US:
                        dv.wait(dve, f"mean{u}", m)
                        dv.did(f"cen{u}", nc.vector.tensor_tensor(heads(t[:, u, :]), heads(x[:, u, :]), spread(mean[:, u, :]), ALU.subtract))
                    for u in US:
                        ac.wait(dve, f"sq{u}", m)
                        dv.did(f"var{u}", nc.vector.reduce_sum(var[:, u, :], heads(sq[:, u, :]), AX.X))
                    for u in US:
                        ac.wait(dve, f"sd{u}", m)
                        dv.did(f"rs{u}", nc.vector.reciprocal(rs[:, u, :], sd[:, u, :]))
                    for u in US:
                        dv.wait(dve, f"rs{u}", m)
                        dv.did(f"nrm{u}", nc.vector.tensor_tensor(heads(t[:, u, :]), heads(t[:, u, :]), spread(rs[:, u, :]), ALU.mult))
                    for u in US:
                        pp.wait(dve, f"g{u}", m)
                        po.wait(dve, f"sum{u}", m)
                        dve.wait_ge(o_out[u], 16 * m + 16)
                        dv.did(f"out{u}", nc.vector.tensor_tensor(o[:, u, :], t[:, u, :], acc[u][:, :], ALU.mult))
                pair_loop(dve, 0, body)


def outproj_phase(nc, sems, tag, d, layer, o_dram, w_dram, src, dst, first=0, subln=None):
    LAMBDA_INIT = 0.8 - 0.6 * math.exp(-0.3)
    US = range(2)
    with ExitStack() as ctx:
        s = Scope(nc, ctx, sems, tag)
        ident = s.sb("ident", [P, P])
        w = s.sb("w", [P, KT, D])
        gate = s.sb("gate", [P, 2, D])
        o, x, t = (s.sb(n, [P, 2, D]) for n in ("o", "x", "t"))
        oT = s.sb("oT", [P, 2, KT, P])
        tr = [[s.ps(f"tr{u}{b}") for b in range(2)] for u in US]
        acc = [[s.ps(f"acc{u}{b}") for b in range(2)] for u in US]
        c_in, w_in, eps_set = s.sem("c_in"), s.sem("w_in"), s.sem("eps_set")
        o_in, x_in, x_out = ([s.sem(f"{n}{u}") for u in US] for n in ("o_in", "x_in", "x_out"))
        pre = subln is not None
        if pre:
            sub, eps = s.sb("sub", [P, P]), s.sb("eps", [P, 1])
            ss, sd, rs = (s.sb(n, [P, 2, CH]) for n in ("ss", "sd", "rs"))
        dv = Rounds(s.sem("dve"), ([f"{n}{u}" for n in ("ss", "rs", "nrm") for u in US] if pre else []) + [f"{n}{b}{u}" for u in US for n in ("g", "x") for b in US])
        ac = Rounds(s.sem("act"), ([f"{n}{u}" for n in ("sq", "sd") for u in US] if pre else []) + [f"T{b}{u}" for u in US for b in US])
        po = Rounds(s.sem("pool"), [f"sub{u}" for u in US])
        pp = Rounds(s.sem("pe"), [f"T{b}{u}" for u in US for b in US] + [f"o{b}{u}" for u in US for b in US])
        heads = lambda z: z.rearrange("p (h c) -> p h c", c=P)
        spread = lambda z: z.rearrange("p (h o) -> p h o", o=1).to_broadcast([P, CH, P])
        nc_in = 3 + (1 if pre else 0)
        rounds = (NT - first) // 2

        with nc.Block() as block:
            @block.sync
            def _(sp):
                sp.dma_start(ident[:, :], d["ident"]).then_inc(c_in, 16)
                for c in range(2):
                    sp.dma_start(gate[:, c, :], row_of(d["mods"][layer, c, GATE1 * D:(GATE1 + 1) * D])).then_inc(c_in, 16)
                if pre:
                    sp.dma_start(sub[:, :], row_of(subln)).then_inc(c_in, 16)

                def body(i, m, _c):
                    for u in US:
                        rows = ds(i * (2 * P) + u * P, P)
                        if not is0(m):
                            pp.wait(sp, f"T1{u}", m - 1)
                        sp.dma_start(o[:, u, :], o_dram[rows, :]).then_inc(o_in[u], 16)
                        if not is0(m):
                            sp.wait_ge(x_out[u], 16 * m)
                        sp.dma_start(x[:, u, :], src[rows, :]).then_inc(x_in[u], 16)
                    if is0(m):
                        for k in range(KT):
                            sp.dma_start(w[:, k, :], w_dram[k * P:(k + 1) * P, :]).then_inc(w_in, 16)
                pair_loop(sp, first, body)

            if pre:
                @block.gpsimd
                def _(pool):
                    pool.wait_ge(c_in, 16 * nc_in)

                    def body(i, m, _c):
                        for u in US:
                            dv.wait(pool, f"nrm{u}", m)
                            po.did(f"sub{u}", nc.gpsimd.tensor_tensor(heads(o[:, u, :]), heads(o[:, u, :]),
                                                                      sub[:, :].rearrange("p (o n) -> p o n", o=1).to_broadcast([P, CH, P]), ALU.mult))
                    pair_loop(pool, first, body)

            @block.tensor
            def _(pe):
                pe.wait_ge(c_in, 16 * nc_in)
                pe.wait_ge(w_in, 16 * KT)

                def body(i, m, _c):
                    for u in US:
                        if pre:
                            po.wait(pe, f"sub{u}", m)
                        else:
                            pe.wait_ge(o_in[u], 16 * m + 16)
                        for b in US:
                            if not is0(m):
                                ac.wait(pe, f"T{b}{u}", m - 1)
                            for k in range(4):
                                x_ = nc.tensor.transpose(tr[u][b][:, k * P:(k + 1) * P], o[:, u, (4 * b + k) * P:(4 * b + k + 1) * P], ident[:, :])
                            pp.did(f"T{b}{u}", x_)
                    for u in US:
                        ac.wait(pe, f"T1{u}", m)
                        for b in US:
                            if not is0(m):
                                dv.wait(pe, f"g{b}{u}", m - 1)
                            for k in range(KT):
                                x_ = nc.tensor.matmul(acc[u][b][:, :], oT[:, u, k, :], w[:, k, b * 512:(b + 1) * 512], start=k == 0, stop=k == KT - 1)
                            pp.did(f"o{b}{u}", x_)
                pair_loop(pe, first, body)

            @block.scalar
            def _(act):
                if pre:
                    act.wait_ge(eps_set, 1)

                def body(i, m, _c):
                    if pre:
                        for u in US:
                            act.wait_ge(o_in[u], 16 * m + 16)
                            if not is0(m):
                                act.wait_ge(x_out[u], 16 * m)
                            ac.did(f"sq{u}", nc.scalar.activation(t[:, u, :], o[:, u, :], ACT.Square))
                        for u in US:
                            dv.wait(act, f"ss{u}", m)
                            ac.did(f"sd{u}", nc.scalar.activation(sd[:, u, :], ss[:, u, :], ACT.Sqrt, scale=1.0 / P, bias=eps[:, 0:1]))
                    for u in US:
                        for b in US:
                            pp.wait(act, f"T{b}{u}", m)
                            if not is0(m):
                                pp.wait(act, f"o1{u}", m - 1)
                            ac.did(f"T{b}{u}", nc.scalar.activation(oT[:, u, 4 * b:4 * b + 4, :], tr[u][b][:, :].rearrange("p (k t) -> p k t", k=4), ACT.Copy))
                    for u in US:
                        dv.wait(act, f"x1{u}", m)
                        act.dma_start(dst[ds(i * (2 * P) + u * P, P), :], x[:, u, :]).then_inc(x_out[u], 16)
                pair_loop(act, first, body)
                for u in US:
                    act.wait_ge(x_out[u], 16 * rounds)

            @block.vector
            def _(dve):
                dve.wait_ge(c_in, 16 * nc_in)
                if pre:
                    nc.vector.memset(eps[:, :], SUBLN_EPS).then_inc(eps_set, 1)
                    nc.vector.tensor_scalar(sub[:, :], sub[:, :], 1.0 - LAMBDA_INIT, None, ALU.mult).then_inc(eps_set, 1)
                    dve.wait_ge(eps_set, 2)

                def body(i, m, cond):
                    if pre:
                        for u in US:
                            ac.wait(dve, f"sq{u}", m)
                            dv.did(f"ss{u}", nc.vector.reduce_sum(ss[:, u, :], heads(t[:, u, :]), AX.X))
                        for u in US:
                            ac.wait(dve, f"sd{u}", m)
                            dv.did(f"rs{u}", nc.vector.reciprocal(rs[:, u, :], sd[:, u, :]))
                        for u in US:
                            dv.wait(dve, f"rs{u}", m)
                            dv.did(f"nrm{u}", nc.vector.tensor_tensor(heads(o[:, u, :]), heads(o[:, u, :]), spread(rs[:, u, :]), ALU.mult))
                    for u in US:
                        for b in US:
                            pp.wait(dve, f"o{b}{u}", m)
                            dv.did(f"g{b}{u}", nc.vector.tensor_tensor(t[:, u, b * 512:(b + 1) * 512], acc[u][b][:, :], gate[:, cond, b * 512:(b + 1) * 512], ALU.mult))
                        dve.wait_ge(x_in[u], 16 * m + 16)
                        for b in US:
                            dv.wait(dve, f"g{b}{u}", m)
                            dv.did(f"x{b}{u}", nc.vector.tensor_tensor(x[:, u, b * 512:(b + 1) * 512], t[:, u, b * 512:(b + 1) * 512], x[:, u, b * 512:(b + 1) * 512], ALU.add))
                pair_loop(dve, first, body)


BR = 64
NPM = (2 * TOK + NE * (BR - 1)) // BR // 2 + 1
NPT = NPM + 1
NBT = 2 * NPT
WR = 3
CAP = TOK // BR
T_NP, T_EXP, T_PEND, T_CODE = 0, 1, 1 + NE, 1 + 2 * NE
T_COLS = T_CODE + NPT


class Chain:

    def __init__(self, eng, sem):
        self.eng, self.sem, self.n = eng, sem, 0

    def did(self, ins):
        ins.then_inc(self.sem, 1)
        self.n += 1
        self.eng.wait_ge(self.sem, self.n)


def route_phase(nc, sems, tag, d, layer, hT, first, slot_dram, slots, gates, tok, table):
    T = NT - first
    TD = NG + NE
    with ExitStack() as ctx:
        s = Scope(nc, ctx, sems, tag)
        wr = s.sb("wr", [P, KT, TD])
        bias = s.sb("bias", [P, TD])
        ident, ones, before, iota = (s.sb(n, [P, P]) for n in ("ident", "ones", "before", "iota"))
        desc = s.sb("desc", [P, EPG])
        tokid = s.sb("tokid", [P, NT])
        zero, steps = s.sb("zero", [P, P]), s.sb("steps", [P, P])
        lgT = s.sb("lgT", [TD, TOK])
        L = s.sb("L", [P, T, TD])
        v1 = s.sb("v1", [P, 16, T])
        g4 = s.sb("g4", [P, 2, T, NG])
        ohg = s.sb("ohg", [P, T, NG])
        big = s.sb("big", [P, T, NG, EPG])
        e8 = s.sb("e8", [P, 2, T, EPG])
        w8 = s.sb("w8", [P, 2, T, EPG])
        oh = s.sb("oh", [P, 2, T, EPG])
        OH = s.sb("OH", [P, 2, T, NE])
        A = s.sb("A", [P, T, NE])
        tb = s.sb("tb", [P, T + 1, NE])
        rank = s.sb("rank", [P, T, NE])
        c32 = s.sb("c32", [P, 8, NE])
        cmp = s.sb("cmp", [P, NBT * NE])
        sf = s.sb("sf", [P, 2, T])
        tf = s.sb("tf", [P, T_COLS])
        bo = s.sb("bo", [P, 2, NBT])
        back = s.sb("back", [NPT, P])
        acc = [s.ps(f"acc{c}") for c in range(3)]
        bankL, bankR, bankT = s.ps("bankL"), s.ps("bankR"), s.ps("bankT")
        c_in, w_in, lg_done, lt_done, l_done, tr_done, exp_in, exp_done = (s.sem(n) for n in (
            "c_in", "w_in", "lg_done", "lt_done", "l_done", "tr_done", "exp_in", "exp_done"))
        a_done, rank_done, slots_done, zeroed, filled, scattered, back_in, back_t, chain, zsem = (s.sem(n) for n in (
            "a_done", "rank_done", "slots_done", "zeroed", "filled", "scattered", "back_in", "back_t", "chain", "zsem"))
        chunks = [(t0, n) for t0, n in ((first * P, 512), (first * P + 512, 512), (first * P + 1024, 256)) if t0 < TOK]
        NC_IN = 16 * 8

        with nc.Block() as block:
            @block.sync
            def _(sp):
                wv = lambda w: w.rearrange("(k p) n -> p k n", p=P)
                sp.dma_start(wr[:, :, 0:NG], wv(d["moe_w_grp"][layer])).then_inc(w_in, 16)
                sp.dma_start(wr[:, :, NG:TD], wv(d["moe_w_rt"][layer])).then_inc(w_in, 16)
                sp.dma_start(ident[:, :], d["ident"]).then_inc(c_in, 16)
                sp.dma_start(ones[:, :], d["ones"]).then_inc(c_in, 16)
                sp.dma_start(before[:, :], d["before"]).then_inc(c_in, 16)
                sp.dma_start(iota[:, :], d["iota"]).then_inc(c_in, 16)
                sp.dma_start(tokid[:, :], d["tokid"]).then_inc(c_in, 16)
                sp.dma_start(bias[:, 0:NG], row_of(d["moe_b_grp"][layer])).then_inc(c_in, 16)
                sp.dma_start(bias[:, NG:TD], row_of(d["moe_b_rt"][layer])).then_inc(c_in, 16)
                sp.dma_start(desc[:, :], d["desc"]).then_inc(c_in, 16)
                sp.wait_ge(zeroed, 1)
                sp.dma_start(slot_dram.rearrange("(n p) o -> n (p o)", p=P), zero[0:NPT, :]).then_inc(filled, 16)
                sp.wait_ge(scattered, 16 * 2 * T)
                sp.dma_start(back[:, :], slot_dram.rearrange("(n p) o -> n (p o)", p=P)).then_inc(back_in, 16)
                sp.wait_ge(back_in, 16)

            @block.gpsimd
            def _(pool):
                nc.gpsimd.memset(zero[:, :], 0.0).then_inc(zeroed, 1)
                pool.wait_ge(filled, 16)
                pool.wait_ge(slots_done, 1)
                pool.wait_ge(c_in, NC_IN)
                for t in range(T):
                    for k in range(2):
                        nc.gpsimd.indirect_dma_start(slot_dram[:, :], bass.IndirectOffsetOnAxis(slots[:, k, t:t + 1], 0),
                                                     tokid[:, first + t:first + t + 1], None).then_inc(scattered, 16)

            @block.tensor
            def _(pe):
                pe.wait_ge(w_in, 32)
                for c, (t0, n) in enumerate(chunks):
                    for k in range(KT):
                        x = nc.tensor.matmul(acc[c][0:TD, 0:n], wr[:, k, :], hT[:, k, t0:t0 + n], start=k == 0, stop=k == KT - 1)
                    x.then_inc(lg_done, 1)
                pe.wait_ge(c_in, NC_IN)
                pe.wait_ge(lt_done, len(chunks))
                for t in range(T):
                    x = nc.tensor.transpose(bankL[:, t * TD:(t + 1) * TD], lgT[:, t * P:(t + 1) * P], ident[0:TD, 0:TD])
                x.then_inc(tr_done, 1)
                pe.wait_ge(a_done, 1)
                rows = A[:, :, :].rearrange("p t e -> p (t e)")
                nc.tensor.matmul(bankR[:, 0:T * NE], before[:, :], rows, start=True, stop=True).then_inc(rank_done, 1)
                nc.tensor.matmul(acc[0][:, 0:T * NE], ones[:, :], rows, start=True, stop=True).then_inc(rank_done, 1)
                pe.wait_ge(back_in, 16)
                nc.tensor.transpose(bankT[:, 0:NPT], back[:, :], ident[0:NPT, 0:NPT]).then_inc(back_t, 1)

            @block.scalar
            def _(act):
                for c, (t0, n) in enumerate(chunks):
                    act.wait_ge(lg_done, c + 1)
                    nc.scalar.activation(lgT[:, c * 512:c * 512 + n], acc[c][0:TD, 0:n], ACT.Copy).then_inc(lt_done, 1)
                act.wait_ge(exp_in, 1)
                nc.scalar.activation(g4[:, 1, :, :], g4[:, 0, :, :], ACT.Exp).then_inc(exp_done, 1)
                act.wait_ge(exp_in, 2)
                nc.scalar.activation(e8[:, 0, :, :], e8[:, 1, :, :], ACT.Exp).then_inc(exp_done, 1)

            @block.vector
            def _(dve):
                V = nc.vector
                c = Chain(dve, chain)
                GM, GSUM, GW, GPICK, EM, M1, M2, PK, SUM, REC, GR = range(11)
                one = lambda i: v1[:, i, :]
                along = lambda i, n: v1[:, i, :].rearrange("p (t o) -> p t o", o=1).to_broadcast([P, T, n])

                def first_of(is_max, weights, scratch, picked, out, n):
                    c.did(V.tensor_tensor(scratch, is_max, weights[:, 0:n].rearrange("p (o e) -> p o e", o=1).to_broadcast([P, T, n]), ALU.mult))
                    c.did(V.tensor_reduce(one(picked), scratch, AX.X, ALU.max))
                    c.did(V.tensor_tensor(out, scratch, along(picked, n), ALU.is_equal))

                dve.wait_ge(c_in, NC_IN)
                dve.wait_ge(tr_done, 1)
                c.did(V.tensor_tensor(L[:, :, :], bankL[:, 0:T * TD].rearrange("p (t e) -> p t e", e=TD),
                                      bias[:, :].rearrange("p (o e) -> p o e", o=1).to_broadcast([P, T, TD]), ALU.add))
                LG = L[:, :, 0:NG]
                c.did(V.tensor_reduce(one(GM), LG, AX.X, ALU.max))
                c.did(V.tensor_tensor(g4[:, 0, :, :], LG, along(GM, NG), ALU.subtract))
                dve.sem_inc(exp_in, 1)
                dve.wait_ge(exp_done, 1)
                c.did(V.reduce_sum(one(GSUM), g4[:, 1, :, :], AX.X))
                c.did(V.reciprocal(one(GW), one(GSUM)))
                c.did(V.tensor_tensor(g4[:, 0, :, :], LG, along(GM, NG), ALU.is_equal))
                first_of(g4[:, 0, :, :], desc, g4[:, 1, :, :], GPICK, ohg[:, :, :], NG)
                group = ohg[:, :, :].rearrange("p t (g o) -> p t g o", o=1).to_broadcast([P, T, NG, EPG])
                c.did(V.tensor_tensor(big[:, :, :, :], L[:, :, NG:TD].rearrange("p t (g e) -> p t g e", e=EPG), group, ALU.mult))
                c.did(V.reduce_sum(w8[:, 0, :, :], big[:, :, :, :].rearrange("p t g e -> p t e g"), AX.X))
                c.did(V.tensor_reduce(one(EM), w8[:, 0, :, :], AX.X, ALU.max))
                c.did(V.tensor_tensor(e8[:, 1, :, :], w8[:, 0, :, :], along(EM, EPG), ALU.subtract))
                dve.sem_inc(exp_in, 1)
                dve.wait_ge(exp_done, 2)
                for k, m in ((0, M1), (1, M2)):
                    c.did(V.tensor_reduce(one(m), e8[:, k, :, :], AX.X, ALU.max))
                    c.did(V.tensor_tensor(w8[:, 0, :, :], e8[:, k, :, :], along(m, EPG), ALU.is_equal))
                    first_of(w8[:, 0, :, :], desc, w8[:, 1, :, :], PK, oh[:, k, :, :], EPG)
                    if k == 0:
                        c.did(V.scalar_tensor_tensor(out=e8[:, 1, :, :], in0=oh[:, 0, :, :], scalar=-2.0, in1=e8[:, 0, :, :], op0=ALU.mult, op1=ALU.add))
                    c.did(V.tensor_tensor(OH[:, k, :, :].rearrange("p t (g e) -> p t g e", e=EPG), group,
                                          oh[:, k, :, :].rearrange("p t (o e) -> p t o e", o=1).to_broadcast([P, T, NG, EPG]), ALU.mult))
                c.did(V.tensor_tensor(A[:, :, :], OH[:, 0, :, :], OH[:, 1, :, :], ALU.add))
                dve.sem_inc(a_done, 1)
                c.did(V.tensor_tensor(one(SUM), one(M1), one(M2), ALU.add))
                c.did(V.reciprocal(one(REC), one(SUM)))
                c.did(V.tensor_tensor(one(GR), one(REC), one(GW), ALU.mult))
                for k, m in ((0, M1), (1, M2)):
                    c.did(V.tensor_tensor(gates[:, k, :], one(m), one(GR), ALU.mult))
                c.did(V.memset(tb[:, 0, :], 0.0))
                dve.wait_ge(rank_done, 2)
                for t in range(T):
                    c.did(V.tensor_tensor(tb[:, t + 1, :], tb[:, t, :], acc[0][:, t * NE:(t + 1) * NE], ALU.add))
                c.did(V.tensor_tensor(rank[:, :, :], bankR[:, 0:T * NE].rearrange("p (t e) -> p t e", e=NE), tb[:, 0:T, :], ALU.add))
                count = tb[:, T, :]
                NB, BEND, BST, USED, UC, ORD, BO, UE = range(8)
                col = lambda i: c32[:, i, :]

                def tally(out, left, right, op, a, b, weight=None):
                    m = cmp[:, 0:a * b].rearrange("p (a b) -> p a b", b=b)
                    c.did(V.tensor_tensor(m, left, right, op))
                    if weight is not None:
                        c.did(V.tensor_tensor(m, m, weight, ALU.mult))
                    c.did(V.reduce_sum(out, m, AX.X))

                rows_ = lambda z, a, b: z.rearrange("p (a o) -> p a o", o=1).to_broadcast([P, a, b])
                cols_ = lambda z, a, b: z.rearrange("p (o b) -> p o b", o=1).to_broadcast([P, a, b])
                c.did(V.tensor_scalar(steps[:, 0:2 * NPT], iota[:, 0:2 * NPT], float(BR), None, ALU.mult))
                tally(col(NB), rows_(count, NE, CAP), cols_(steps[:, 0:CAP], NE, CAP), ALU.is_gt, NE, CAP)
                c.did(V.tensor_tensor_scan(col(BEND), ones[:, 0:NE], col(NB), 0.0, ALU.mult, ALU.add))
                c.did(V.tensor_tensor(col(BST), col(BEND), col(NB), ALU.subtract))
                c.did(V.tensor_scalar(col(BST), col(BST), float(BR), None, ALU.mult))
                c.did(V.tensor_tensor(rank[:, :, :], rank[:, :, :], cols_(col(BST), T, NE), ALU.add))
                for k in range(2):
                    m = cmp[:, 0:T * NE].rearrange("p (t e) -> p t e", e=NE)
                    c.did(V.tensor_tensor(m, rank[:, :, :], OH[:, k, :, :], ALU.mult))
                    c.did(V.reduce_sum(sf[:, k, :], m, AX.X))
                c.did(V.tensor_copy(slots[:, :, :], sf[:, :, :]))
                dve.sem_inc(slots_done, 1)
                c.did(V.tensor_scalar(col(USED), col(NB), 0.0, None, ALU.is_gt))
                c.did(V.tensor_tensor_scan(col(UC), ones[:, 0:NE], col(USED), 0.0, ALU.mult, ALU.add))
                c.did(V.tensor_tensor(col(ORD), col(UC), col(USED), ALU.subtract))
                tally(col(BO), cols_(col(ORD), NE, NE), rows_(iota[:, 0:NE], NE, NE), ALU.is_le, NE, NE, cols_(col(NB), NE, NE))
                c.did(V.tensor_tensor(col(UE), col(USED), iota[:, 0:NE], ALU.mult))
                tally(tf[:, T_EXP:T_EXP + NE], cols_(col(ORD), NE, NE), rows_(iota[:, 0:NE], NE, NE), ALU.is_equal, NE, NE, cols_(col(UE), NE, NE))
                c.did(V.tensor_scalar(steps[:, 0:NPM], iota[:, 0:NPM], 2.0, None, ALU.mult))
                tally(tf[:, T_PEND:T_PEND + NE], rows_(col(BO), NE, NPM), cols_(steps[:, 0:NPM], NE, NPM), ALU.is_gt, NE, NPM)
                c.did(V.tensor_copy(tf[:, T_NP:T_NP + 1], tf[:, T_PEND + NE - 1:T_PEND + NE]))
                tally(bo[:, 0, :], cols_(col(BO), NBT, NE), rows_(iota[:, 0:NBT], NBT, NE), ALU.is_le, NBT, NE)
                c.did(V.tensor_scalar(col(USED)[:, 0:1], col(UC)[:, NE - 1:NE], 1.0, None, ALU.subtract))
                c.did(V.tensor_scalar(bo[:, 0, :], bo[:, 0, :], col(USED)[:, 0:1], None, ALU.min))
                c.did(V.tensor_scalar(steps[:, 0:NE // WR + 1], iota[:, 1:NE // WR + 2], float(WR), None, ALU.mult))
                q = NE // WR + 1
                tally(bo[:, 1, :], rows_(bo[:, 0, :], NBT, q), cols_(steps[:, 0:q], NBT, q), ALU.is_ge, NBT, q)
                c.did(V.scalar_tensor_tensor(out=bo[:, 1, :], in0=bo[:, 1, :], scalar=-float(WR), in1=bo[:, 0, :], op0=ALU.mult, op1=ALU.add))
                code = tf[:, T_CODE:T_CODE + NPT]
                c.did(V.tensor_scalar(code, bo[:, 0, 1:NBT:2], float(WR * WR), float(WR * WR), ALU.mult, ALU.add))
                c.did(V.scalar_tensor_tensor(out=code, in0=bo[:, 1, 0:NBT:2], scalar=float(WR), in1=code, op0=ALU.mult, op1=ALU.add))
                c.did(V.tensor_tensor(code, bo[:, 1, 1:NBT:2], code, ALU.add))
                c.did(V.tensor_copy(table[:, :], tf[0:1, :]))
                dve.wait_ge(back_t, 1)
                c.did(V.tensor_copy(tok[:, :], bankT[:, 0:NPT]))


def experts_phase(nc, sems, tag, d, layer, rows, yb, tok, table, fill):
    WCOLS = 2 * KT * EH + (EH // P) * D
    UP, DOWN = KT * EH, 2 * KT * EH
    HT = EH // P
    with ExitStack() as ctx:
        s = Scope(nc, ctx, sems, tag)
        ident = s.sb("ident", [P, P])
        w = s.sb("w", [P, WR * WCOLS])
        idx = s.sb("idx", [P, 1], U32)
        x = s.sb("x", [P, D])
        xT = s.sb("xT", [P, KT, P])
        sg, a = s.sb("sg", [P, EH]), s.sb("a", [P, EH])
        aT = s.sb("aT", [P, HT, P])
        y = s.sb("y", [P, D])
        tr = [s.ps(f"tr{b}") for b in range(2)]
        bG, bU, bA = s.ps("bG"), s.ps("bU"), s.ps("bA")
        bY = [s.ps(f"bY{b}") for b in range(2)]
        c_in, idx_done, x_in, xtr, xT_done = (s.sem(n) for n in (
            "c_in", "idx_done", "x_in", "xtr", "xT_done"))
        w_in = [[s.sem(f"w_in{part}{u}") for u in range(WR)] for part in ("gate", "up", "down")]
        w_ready = [s.sem(f"w_ready_{part}") for part in ("gate", "up", "down")]
        g_done, u_done, sg_done, a_done, atr, aT_done, y_done, ye_act, ye_dve, y_out = (s.sem(n) for n in (
            "g_done", "u_done", "sg_done", "a_done", "atr", "aT_done", "y_done", "ye_act", "ye_dve", "y_out"))
        go, ended, filled, zeroed = (s.sem(n) for n in ("go", "ended", "filled", "zeroed"))
        zero = s.sb("zero", [P, D])
        wv = lambda name: d[name][layer].rearrange("e (k p) n -> p e k n", p=P)

        def load(eng, col, most, least=0):
            return eng.value_load(table[0:1, col], min_val=least, max_val=most)

        with nc.Block() as block:
            @block.sync
            def _(sp):
                sp.dma_start(ident[:, :], d["ident"]).then_inc(c_in, 16)

                def fetch(u, e, tiles, part):
                    if tiles is not None:
                        sp.wait_ge((g_done, u_done, y_done)[part], (1, 1, 2)[part] * tiles)
                    name, at, kk, n = (("moe_w_gate", 0, KT, EH), ("moe_w_up", UP, KT, EH), ("moe_w_down", DOWN, HT, D))[part]
                    sp.dma_start(w[:, u * WCOLS + at:u * WCOLS + at + kk * n].rearrange("p (o k n) -> p o k n", o=1, n=n),
                                 wv(name)[:, ds(e, 1), :, :]).then_inc(w_in[part][u], 16)

                def arrived(u, times, part):
                    sp.wait_ge(w_in[part][u], 16 * times)
                    sp.sem_inc(w_ready[part], 1)

                def step(o, u, free, before):
                    e = load(sp, ds(o + T_EXP, 1), NE - 1)
                    tiles = load(sp, ds(o + (T_PEND - WR), 1), NPM, 1) if free else None
                    for part in range(3):
                        fetch(u, e, tiles, part)
                        if before is not None:
                            arrived(*before, part)

                for o in range(WR):
                    step(o, o, False, (o - 1, 1) if o else None)
                if fill:
                    sp.wait_ge(zeroed, 1)
                    n = load(sp, slice(T_NP, T_NP + 1), NPM)
                    with sp.Fori(n, NPT) as i:
                        sp.dma_start(yb[ds(i * P, P), :], zero[:, :]).then_inc(filled, 16)
                with sp.Fori(1, NE // WR) as i:
                    for u in range(WR):
                        step(WR * i + u, u, True, (u - 1, i + 1) if u else (WR - 1, i))
                left = NE % WR
                for u in range(left):
                    step(NE - left + u, u, True, (u - 1, NE // WR + 1) if u else (WR - 1, NE // WR))
                for part in range(3):
                    arrived((NE - 1) % WR, (NE - 1) // WR + 1, part)
                if fill:
                    with sp.Fori(0, n) as i:
                        sp.sem_inc(filled, 16)
                    sp.wait_ge(filled, 16 * NPT)
                    sp.sem_inc(ended, 1)

            @block.gpsimd
            def _(pool):
                nc.gpsimd.memset(zero[:, :], 0.0).then_inc(zeroed, 1)
                n = load(pool, slice(T_NP, T_NP + 1), NPM)
                nc.gpsimd.tensor_copy(idx[:, :], tok[:, 0:1]).then_inc(idx_done, 1)
                pool.wait_ge(idx_done, 1)
                nc.gpsimd.indirect_dma_start(x[:, :], None, rows[:, :], bass.IndirectOffsetOnAxis(idx[:, 0:1], 0)).then_inc(x_in, 16)
                with pool.Fori(0, n) as i:
                    pool.wait_ge(x_in, 16 * i + 16)
                    nc.gpsimd.tensor_copy(idx[:, :], tok[:, ds(i + 1, 1)]).then_inc(idx_done, 1)
                    pool.wait_ge(idx_done, i + 2)
                    pool.wait_ge(xtr, 2 * i + 2)
                    pool.sem_inc(go, 1)
                    nc.gpsimd.indirect_dma_start(x[:, :], None, rows[:, :], bass.IndirectOffsetOnAxis(idx[:, 0:1], 0)).then_inc(x_in, 16)

            @block.tensor
            def _(pe):
                pe.wait_ge(c_in, 16)
                n = load(pe, slice(T_NP, T_NP + 1), NPM)

                def turn(i, again):
                    pe.wait_ge(x_in, 16 * i + 16)
                    for b in range(2):
                        if again:
                            pe.wait_ge(xT_done, 2 * i - 1 + b)
                        for k in range(4):
                            t = nc.tensor.transpose(tr[b][:, k * P:(k + 1) * P], x[:, (4 * b + k) * P:(4 * b + k + 1) * P], ident[:, :])
                        t.then_inc(xtr, 1)

                turn(0, False)
                with pe.Fori(0, n) as i:
                    code = load(pe, ds(i + T_CODE, 1), WR * WR * (NE + 1) - 1, WR * WR)
                    need, slot1 = code // (WR * WR), code % WR
                    slot0 = (code % (WR * WR)) // WR * WCOLS

                    def products(bank, stationary, tiles, offset, n, done):
                        for u in range(WR):
                            with pe.If(slot1 == u):
                                for k in range(tiles):
                                    nc.tensor.matmul(bank[0:BR, :], stationary[:, k, 0:BR], w[:, ds(slot0 + (offset + k * n), 512)],
                                                     start=k == 0, stop=k == tiles - 1)
                                    at = u * WCOLS + offset + k * n
                                    m = nc.tensor.matmul(bank[BR:P, :], stationary[:, k, BR:P], w[:, at:at + 512], start=k == 0, stop=k == tiles - 1)
                                m.then_inc(done, 1)

                    pe.wait_ge(w_ready[0], need)
                    pe.wait_ge(xT_done, 2 * i + 2)
                    products(bG, xT, KT, 0, EH, g_done)
                    pe.wait_ge(w_ready[1], need)
                    products(bU, xT, KT, UP, EH, u_done)
                    turn(i + 1, True)
                    pe.wait_ge(a_done, i + 2)
                    for k in range(HT):
                        t = nc.tensor.transpose(bA[:, k * P:(k + 1) * P], a[:, k * P:(k + 1) * P], ident[:, :])
                    t.then_inc(atr, 1)
                    pe.wait_ge(aT_done, i + 1)
                    pe.wait_ge(ye_act, i + 1)
                    pe.wait_ge(ye_dve, i + 1)
                    pe.wait_ge(w_ready[2], need)
                    for b in range(2):
                        products(bY[b], aT, HT, DOWN + b * 512, D, y_done)

            @block.scalar
            def _(act):
                n = load(act, slice(T_NP, T_NP + 1), NPM)
                act.sem_inc(ye_act, 1)
                act.sem_inc(y_out, 16)

                def turned(i):
                    for b in range(2):
                        act.wait_ge(xtr, 2 * i + b + 1)
                        nc.scalar.activation(xT[:, 4 * b:4 * b + 4, :], tr[b][:, :].rearrange("p (k t) -> p k t", k=4), ACT.Copy).then_inc(xT_done, 1)
                turned(0)
                with act.Fori(0, n) as i:
                    act.wait_ge(g_done, i + 1)
                    act.wait_ge(a_done, i + 1)
                    nc.scalar.activation(sg[:, :], bG[:, :], ACT.Silu).then_inc(sg_done, 1)
                    turned(i + 1)
                    act.wait_ge(y_done, 2 * i + 1)
                    act.wait_ge(y_out, 16 * i + 16)
                    nc.scalar.activation(y[:, 0:512], bY[0][:, :], ACT.Copy).then_inc(ye_act, 1)
                    act.wait_ge(ye_act, i + 2)
                    act.wait_ge(ye_dve, i + 2)
                    act.dma_start(yb[ds(i * P, P), :], y[:, :]).then_inc(y_out, 16)
                act.wait_ge(y_out, 16 * n + 16)
                act.sem_inc(ended, 1)

            @block.vector
            def _(dve):
                n = load(dve, slice(T_NP, T_NP + 1), NPM)
                dve.sem_inc(ye_dve, 1)
                dve.sem_inc(a_done, 1)
                with dve.Fori(0, n) as i:
                    dve.wait_ge(sg_done, i + 1)
                    dve.wait_ge(u_done, i + 1)
                    nc.vector.tensor_tensor(a[:, :], sg[:, :], bU[:, :], ALU.mult).then_inc(a_done, 1)
                    dve.wait_ge(atr, i + 1)
                    nc.vector.tensor_copy(aT[:, :, :], bA[:, :].rearrange("p (k t) -> p k t", k=HT)).then_inc(aT_done, 1)
                    dve.wait_ge(y_done, 2 * i + 2)
                    dve.wait_ge(y_out, 16 * i + 16)
                    nc.vector.tensor_copy(y[:, 512:1024], bY[1][:, :]).then_inc(ye_dve, 1)


def combine_phase(nc, sems, tag, d, layer, yb, src, dst, slots, gates, first=0, final_gain=None):
    US = range(2)
    fin = final_gain is not None
    with ExitStack() as ctx:
        s = Scope(nc, ctx, sems, tag)
        gate = s.sb("gate", [P, 2, D])
        fg, eps = s.sb("fg", [P, D]), s.sb("eps", [P, 1])
        idx = s.sb("idx", [P, 2, 2, 1], U32)
        yr = s.sb("yr", [P, 2, 2, D])
        x, t, sq = (s.sb(n, [P, 2, D]) for n in ("x", "t", "sq"))
        ss, sd, rs = (s.sb(n, [P, 2]) for n in ("ss", "sd", "rs"))
        gt = s.sb("gt", [P, 2, 2])
        c_in, eps_set = s.sem("c_in"), s.sem("eps_set")
        y_in, x_in, x_out = ([s.sem(f"{n}{u}") for u in US] for n in ("y_in", "x_in", "x_out"))
        po = Rounds(s.sem("pool"), [f"idx{u}" for u in US] + [f"mod{u}" for u in US])
        dv = Rounds(s.sem("dve"), [f"{n}{u}" for u in US for n in ("g", "a", "b")] + [f"x{u}" for u in US] + ([f"{n}{u}" for n in ("rs", "out") for u in US] if fin else []))
        ac = Rounds(s.sem("act"), [f"{n}{u}" for n in ("ss", "sd") for u in US])
        go = s.sem("go")
        last_name = "out" if fin else "x"
        rounds = (NT - first) // 2

        with nc.Block() as block:
            @block.sync
            def _(sp):
                for c in range(2):
                    sp.dma_start(gate[:, c, :], row_of(d["mods"][layer, c, GATE2 * D:(GATE2 + 1) * D])).then_inc(c_in, 16)
                if fin:
                    sp.dma_start(fg[:, :], row_of(final_gain)).then_inc(c_in, 16)

                def body(i, m, _c):
                    for u in US:
                        if not is0(m):
                            sp.wait_ge(x_out[u], 16 * m)
                        sp.dma_start(x[:, u, :], src[ds(i * (2 * P) + u * P, P), :]).then_inc(x_in[u], 16)
                pair_loop(sp, first, body)

            @block.gpsimd
            def _(pool):
                pool.wait_ge(c_in, 16 * (3 if fin else 2))

                def body(i, m, cond):
                    for u in US:
                        if not is0(m):
                            pool.wait_ge(y_in[u], 32 * m)
                        po.did(f"idx{u}", nc.gpsimd.tensor_copy(idx[:, u, :, :], slots[:, :, ds(i * 2 + (u - first), 1)]))
                    for u in US:
                        po.wait(pool, f"idx{u}", m)
                        if not is0(m):
                            dv.wait(pool, f"b{u}", m - 1)
                        pool.sem_inc(go, 1)
                        for k in range(2):
                            nc.gpsimd.indirect_dma_start(yr[:, u, k, :], None, yb[:, :], bass.IndirectOffsetOnAxis(idx[:, u, k, :], 0)).then_inc(y_in[u], 16)
                    for u in US:
                        dv.wait(pool, f"b{u}", m)
                        po.did(f"mod{u}", nc.gpsimd.tensor_tensor(t[:, u, :], t[:, u, :], gate[:, cond, :], ALU.mult))
                pair_loop(pool, first, body)

            @block.vector
            def _(dve):
                nc.vector.memset(eps[:, :], RMS_EPS).then_inc(eps_set, 1)
                dve.wait_ge(c_in, 16 * (3 if fin else 2))

                def body(i, m, cond):
                    for u in US:
                        dve.wait_ge(y_in[u], 32 * m + 32)
                        if not is0(m):
                            dv.wait(dve, f"x{u}", m - 1)
                        dv.did(f"g{u}", nc.vector.tensor_copy(gt[:, u, :], gates[:, :, ds(i * 2 + (u - first), 1)].rearrange("p k o -> p (k o)")))
                        dv.wait(dve, f"g{u}", m)
                        dv.did(f"a{u}", nc.vector.tensor_scalar(t[:, u, :], yr[:, u, 0, :], gt[:, u, 0:1], None, ALU.mult))
                        dv.wait(dve, f"a{u}", m)
                        dv.did(f"b{u}", nc.vector.scalar_tensor_tensor(out=t[:, u, :], in0=yr[:, u, 1, :], scalar=gt[:, u, 1:2], in1=t[:, u, :], op0=ALU.mult, op1=ALU.add))
                    for u in US:
                        po.wait(dve, f"mod{u}", m)
                        dve.wait_ge(x_in[u], 16 * m + 16)
                        dv.did(f"x{u}", nc.vector.tensor_tensor(x[:, u, :], x[:, u, :], t[:, u, :], ALU.add))
                    if fin:
                        for u in US:
                            ac.wait(dve, f"sd{u}", m)
                            dv.did(f"rs{u}", nc.vector.reciprocal(rs[:, u:u + 1], sd[:, u:u + 1]))
                        for u in US:
                            dv.wait(dve, f"rs{u}", m)
                            dv.did(f"out{u}", nc.vector.scalar_tensor_tensor(out=x[:, u, :], in0=x[:, u, :], scalar=rs[:, u:u + 1], in1=fg[:, :], op0=ALU.mult, op1=ALU.mult))
                pair_loop(dve, first, body)

            @block.scalar
            def _(act):
                act.wait_ge(eps_set, 1)

                def body(i, m, _c):
                    if fin:
                        for u in US:
                            dv.wait(act, f"x{u}", m)
                            if not is0(m):
                                dv.wait(act, f"rs{u}", m - 1)
                            ac.did(f"ss{u}", nc.scalar.activation(sq[:, u, :], x[:, u, :], ACT.Square, accum_out=ss[:, u:u + 1]))
                        for u in US:
                            ac.wait(act, f"ss{u}", m)
                            ac.did(f"sd{u}", nc.scalar.activation(sd[:, u:u + 1], ss[:, u:u + 1], ACT.Sqrt, scale=1.0 / D, bias=eps[:, 0:1]))
                    for u in US:
                        dv.wait(act, f"{last_name}{u}", m)
                        act.dma_start(dst[ds(i * (2 * P) + (u - (first if fin else 0)) * P, P), :], x[:, u, :]).then_inc(x_out[u], 16)
                pair_loop(act, first, body)
                for u in US:
                    act.wait_ge(x_out[u], 16 * rounds)



CONSTS = ("cos", "sin", "ident", "ones", "blockones", "headones", "headcols", "tri", "first", "levels", "before", "iota", "tokid", "desc")


def build(nc, d, out):
    def dram(name, shape, dt=F32):
        return nc.dram_tensor(name, shape, dt).ap()

    d["mods"] = dram("mods_dram", (2, 2, MODS))
    projT = dram("projT_dram", (3 * D, TOK))
    qT, kT, h, o, y = dram("qT_dram", (D, TOK)), dram("kT_dram", (D, TOK)), dram("h_dram", (TOK, D)), dram("o_dram", (TOK, D)), dram("y_dram", (TOK, BW))
    x0, x1, x2, x3 = (dram(f"x{i}_dram", (TOK, D)) for i in range(4))
    slot_dram, yb = dram("slot_dram", (NPT * P, 1)), dram("yb_dram", (NPT * P, D))
    sems = None

    def static(ctx, name, shape, dt=F32):
        return ctx.enter_context(nc.sbuf_tensor(name, shape, dt))

    def load_keys(ctx, tag, K, tiles):
        with ExitStack() as inner:
            s = Scope(nc, inner, sems, tag)
            k_in = s.sem("k_in")
            with nc.Block() as block:
                @block.sync
                def _(sp):
                    for i in range(tiles):
                        sp.dma_start(K[:, i, :], kT[i * P:(i + 1) * P, :]).then_inc(k_in, 16)
                    sp.wait_ge(k_in, 16 * tiles)

    def moe(layer, src_rows, dst, first, gain):
        with ExitStack() as ctx:
            T = NT - first
            slots, tok = static(ctx, f"slots{layer}", [P, 2, T], U32), static(ctx, f"tok{layer}", [P, NPT], U32)
            gates, table = static(ctx, f"gates{layer}", [P, 2, T]), static(ctx, f"table{layer}", [1, T_COLS], I32)
            with ExitStack() as inner:
                hT = static(inner, f"hT_moe{layer}", [P, KT, TOK])
                norm_phase(nc, sems, f"nb{layer}", d, layer, SHIFT2, src_rows, hT, d["ident"], rows_out=h, first=first)
                route_phase(nc, sems, f"rt{layer}", d, layer, hT, first, slot_dram, slots, gates, tok, table)
            experts_phase(nc, sems, f"ex{layer}", d, layer, h, yb, tok, table, fill=layer == 0)
            combine_phase(nc, sems, f"cb{layer}", d, layer, yb, src_rows, dst, slots, gates, first, gain)

    mods_phase(nc, sems, d, x0)

    with ExitStack() as ctx:
        hT = static(ctx, "hT0", [P, KT, TOK], F32R), static(ctx, "hT0_rest", [P, KT, TOK], F32R)
        norm_phase(nc, sems, "n0", d, 0, SHIFT1, x0, hT, d["ident"])
        proj_phase(nc, sems, "p0", d["ev_w_in"][0], hT, projT)
    with ExitStack() as ctx:
        V, K = static(ctx, "V0", [P, NT, AKW]), static(ctx, "K0", [P, AKV, TOK])
        gqa_qk(nc, sems, d, projT, qT, kT, V)
        load_keys(ctx, "k0", K, AKV)
        kv_of = lambda pair: pair // 2
        attn_phase(nc, sems, "al", d, qT, kv_of, K, V, o, AH // 2, CT, NT - CT, NT, False)
        attn_phase(nc, sems, "ac", d, qT, kv_of, K, V, o, AH // 2, 0, CT, CT, False)
    with ExitStack() as ctx:
        lora, gate = static(ctx, "lora", [P, GAP]), static(ctx, "gate", [P, GAP])
        vtok, srk = static(ctx, "vtok", [P, NT, BW]), static(ctx, "srk", [P, NT, BH])
        rwkv_shared_phase(nc, sems, d, projT, lora, gate)
        for j in range(BH // 2):
            with ExitStack() as inner:
                kr, bk = static(inner, f"kr{j}", [P, 2, 2, GAP]), static(inner, f"bk{j}", [P, 2, 2, GAP])
                last, vflip = static(inner, f"last{j}", [P, 2, NCK]), static(inner, f"vflip{j}", [P, NCK, HD])
                rwkv_prep_phase(nc, sems, j, d, projT, lora, kr, bk, last, vflip, vtok, srk)
                rwkv_scan_phase(nc, sems, j, d, kr, bk, last, vflip, y)
        readout_phase(nc, sems, d, y, gate, vtok, srk, o)
    outproj_phase(nc, sems, "o0", d, 0, o, d["ev_w_out"][0], x0, x1)
    moe(0, x1, x2, 0, None)

    with ExitStack() as ctx:
        hT = static(ctx, "hT1", [P, KT, TOK], F32R), static(ctx, "hT1_rest", [P, KT, TOK], F32R)
        norm_phase(nc, sems, "n1", d, 1, SHIFT1, x2, hT, d["ident"])
        proj_phase(nc, sems, "p1", d["od_w_in"][0], hT, projT)
    with ExitStack() as ctx:
        V = static(ctx, "V1", [P, NT, D])
        def tile_rows(base):
            return lambda j, u: [projT[ds(j * (2 * P) + base + u * P, P), :]]
        qk_phase(nc, sems, "dqk", d, projT,
                 [(CH, tile_rows(0), lambda j, u: qT[ds(j * (2 * P) + u * P, P), :], 0),
                  (CH, tile_rows(D), lambda j, u: kT[ds(j * (2 * P) + u * P, P), :], 1)], [2 * D // P + i for i in range(CH)], V)
        K = static(ctx, "K1", [P, CH, TOK])
        load_keys(ctx, "k1", K, CH)
        attn_phase(nc, sems, "ad", d, qT, lambda pair: pair, K, V, o, CH, CT, NT - CT, NT, True)
    outproj_phase(nc, sems, "o1", d, 1, o, d["od_w_out"][0], x2, x3, CT, d["od_subln"][0])
    moe(1, x3, out, CT, d["final_gain"])


def shape_constants():
    f = np.float32
    nf = HD // 4
    inv = (ROPE_THETA ** (-np.arange(nf, dtype=f) / f(nf))).astype(f)
    t = np.arange(SEQ)
    angle = np.concatenate([(t // GRID_W).astype(f)[:, None] * inv, (t % GRID_W).astype(f)[:, None] * inv], axis=1)
    c = np.arange(P) % HD
    at = (c // 32) * nf + c % nf
    sign = np.where(c % 32 < nf, -1.0, 1.0).astype(f)
    p = np.arange(P)
    head, pos = p // HD, p % HD
    same = head[:, None] == head[None]
    tri = np.zeros((P, 2, 2, 2, P), f)
    for dr in range(2):
        s, u = pos[:, None], pos[None]
        strict, whole = ((s < u), (s <= u)) if dr == 0 else ((s > u), (s >= u))
        tri[:, dr, 0, 0], tri[:, dr, 0, 1] = strict & same, strict & ~same
        tri[:, dr, 1, 0], tri[:, dr, 1, 1] = -1.0 * (whole & same), whole & ~same
    levels = np.zeros((P, 6, P), f)
    for l in range(6):
        b = 1 << l
        levels[:, l] = same & (pos[:, None] // (2 * b) == pos[None] // (2 * b)) & (pos[:, None] // b != pos[None] // b)
    return {
        "cos": np.cos(angle).astype(f).T[at].copy(),
        "sin": (np.sin(angle).astype(f).T[at] * sign[:, None]).astype(f),
        "ident": np.eye(P, dtype=f),
        "ones": np.ones((P, P), f),
        "blockones": same.astype(f) / HD,
        "headones": same.astype(f),
        "headcols": (head[:, None] == np.arange(2)[None]).astype(f),
        "tri": tri,
        "first": np.stack([-tri[:, :, 0, 0] * levels[:, 0:1], tri[:, :, 0, 0] * levels[:, 1:2]], axis=1),
        "levels": levels,
        "before": (p[:, None] < p[None]).astype(f),
        "iota": np.tile(p[None], (P, 1)).astype(f),
        "tokid": (np.arange(NT)[None] * P + p[:, None]).astype(f),
        "desc": np.tile(EPG - np.arange(EPG)[None], (P, 1)).astype(f),
    }


_INS = ["x", "c", "ctx", "c_ctx", "mod_w", "mod_b", "ev_w_in", "ev_w_out", "ev_q_gain", "ev_k_gain", "ev_mu_prev", "ev_mu_next",
        "ev_w0", "ev_w2", "ev_a0", "ev_a2", "ev_g2", "ev_k_k", "ev_k_a", "ev_r_k", "ev_gn_w", "ev_gn_b", "od_w_in", "od_w_out",
        "od_lq1", "od_lk1", "od_lq2", "od_lk2", "od_subln", "moe_w_grp", "moe_b_grp", "moe_w_rt", "moe_b_rt", "moe_w_gate",
        "moe_w_up", "moe_w_down", "final_gain"]


def kernel(**inputs):
    import concourse.bacc as _bacc
    from concourse.bass_utils import run_bass_kernel_spmd as _run

    nc = _bacc.Bacc("TRN2", target_bir_lowering=False, num_devices=1)
    arrays, d = {}, {}
    values = {name: inputs[name] for name in _INS}
    values.update(shape_constants())
    for name, value in values.items():
        a = np.ascontiguousarray(value)
        arrays[f"in_{name}"] = a
        d[name] = nc.dram_tensor(f"in_{name}", a.shape, mybir.dt.from_np(a.dtype), kind="ExternalInput").ap()
    out = nc.dram_tensor("out_rows", (SEQ, D), F32, kind="ExternalOutput").ap()
    with nc.allow_non_contiguous_dma(reason="columns of weights and per-channel vectors"):
        build(nc, d, out)
    r = _run(nc, [arrays], core_ids=[0])
    return r.results[0]["out_rows"].reshape(1, SEQ, D)
```
